# Optimizing a Trainium2 kernel written in Bass

```python
import jax
import jax.numpy as jnp
from jax import lax
import numpy as np

D_MODEL = 1024
BATCH = 1
SEQ = 512
DEPTH = 2

CHUNK = 64
PLE_DIM = 256
D_FF = 2816
RW_HEADS = 8
RW_HEAD_DIM = 64
RW_WIDTH = RW_HEADS * RW_HEAD_DIM
RW_CHUNK = CHUNK
RW_DECAY_LORA = 64
RW_AAA_LORA = 64
RW_GATE_LORA = 160
RW_GN_EPS = 64e-5
SB_HEADS = 4
SB_HEAD_DIM = 128
SB_WIDTH = SB_HEADS * SB_HEAD_DIM
SB_BLOCK = 128
HG_HEADS = 4
HG_EXPAND = 128
HG_HEAD_V = 128
HG_FWIDTH = HG_HEADS * HG_EXPAND
HG_VWIDTH = HG_HEADS * HG_HEAD_V
HG_CHUNK = 16
HG_EPS = 1e-5
N_BRANCH = 3
LN_EPS = 1e-5
ALPHA = (2 * DEPTH) ** 0.25
BETA = (8 * DEPTH) ** -0.25

RW_SPLITS = [RW_WIDTH, RW_WIDTH, RW_WIDTH, RW_DECAY_LORA, RW_AAA_LORA, RW_GATE_LORA]
RW_COLS = sum(RW_SPLITS)
SB_COLS = 3 * SB_WIDTH
HG_SPLITS = [HG_FWIDTH, HG_FWIDTH, HG_VWIDTH, HG_VWIDTH]
HG_COLS = sum(HG_SPLITS)
GATE_COLS = N_BRANCH * D_MODEL
IN_SPLITS = [RW_COLS, SB_COLS, HG_COLS, GATE_COLS]
IN_COLS = sum(IN_SPLITS)

kernel_name = "hybrid_rwkv7_stickbreak_hgrn2_macaron_deepnorm"

def split_cols(u, sizes):
    idx = np.cumsum(sizes)[:-1].tolist()
    return jnp.split(u, idx, axis=-1)

def heads(t, n_heads):
    b, s, c = t.shape
    return t.reshape(b, s, n_heads, c // n_heads)

def layer_norm(x, g, b):
    xf = x.astype(jnp.float32)
    mu = jnp.mean(xf, axis=-1, keepdims=True)
    var = jnp.mean(jnp.square(xf - mu), axis=-1, keepdims=True)
    return ((xf - mu) * lax.rsqrt(var + LN_EPS) * g + b).astype(x.dtype)

def head_norm(y, g, b, eps):
    mu = jnp.mean(y, axis=-1, keepdims=True)
    var = jnp.mean(jnp.square(y - mu), axis=-1, keepdims=True)
    y = ((y - mu) * lax.rsqrt(var + eps)).reshape(y.shape[:2] + (-1,))
    return y * g + b

def head_rms_norm(y, g, eps):
    y = y * lax.rsqrt(jnp.mean(jnp.square(y), axis=-1, keepdims=True) + eps)
    return y.reshape(y.shape[:2] + (-1,)) * g

def swiglu(h, wg, wu, wd):
    return (jax.nn.silu(h @ wg) * (h @ wu)) @ wd

def token_shift(u):
    return jnp.pad(u[:, :-1], ((0, 0), (1, 0), (0, 0)))

def rwkv7_chunked(r, log_w, k, v, a, b):
    bsz, seq, nh, n = r.shape
    nc = seq // RW_CHUNK
    f32 = jnp.float32

    def chunks(t):
        return t.astype(f32).reshape(bsz, nc, RW_CHUNK, nh, n).transpose(0, 1, 3, 2, 4)

    r, log_w, k, v, a, b = (chunks(t) for t in (r, log_w, k, v, a, b))
    g = jnp.cumsum(log_w, axis=3)
    g_last = g[..., -1:, :]
    inv = jnp.exp(-g)
    a_dec = a * jnp.exp(g - log_w)
    r_dec = r * jnp.exp(g)
    b_inv = b * inv
    k_inv = k * inv
    strict = jnp.tril(jnp.ones((RW_CHUNK, RW_CHUNK), bool), -1)
    incl = jnp.tril(jnp.ones((RW_CHUNK, RW_CHUNK), bool))

    def pair(x_t, y_s, mask):
        return jnp.where(mask, jnp.einsum('bnhtk,bnhsk->bnhts', x_t, y_s), 0.0)

    L_ab = pair(a_dec, b_inv, strict)
    L_ak = pair(a_dec, k_inv, strict)
    M_rb = pair(r_dec, b_inv, incl)
    M_rk = pair(r_dec, k_inv, incl)
    lhs = jnp.eye(RW_CHUNK, dtype=f32) - L_ab
    W1 = lax.linalg.triangular_solve(lhs, a_dec, left_side=True, lower=True, unit_diagonal=True)
    U0 = lax.linalg.triangular_solve(lhs, jnp.einsum('bnhts,bnhsv->bnhtv', L_ak, v),
                                     left_side=True, lower=True, unit_diagonal=True)
    Q_eff = r_dec + jnp.einsum('bnhts,bnhsk->bnhtk', M_rb, W1)
    Y_intra = jnp.einsum('bnhts,bnhsv->bnhtv', M_rb, U0) + jnp.einsum('bnhts,bnhsv->bnhtv', M_rk, v)
    dec = jnp.exp(g_last - g)
    b_dec = b * dec
    k_dec = k * dec
    P = jnp.einsum('bnhck,bnhcj->bnhkj', W1, b_dec) + jnp.exp(g_last)[..., 0, :, None] * jnp.eye(n, dtype=f32)
    D = jnp.einsum('bnhcv,bnhcj->bnhvj', U0, b_dec) + jnp.einsum('bnhcv,bnhcj->bnhvj', v, k_dec)

    def step(S, inp):
        P_c, D_c = inp
        return jnp.einsum('bhvk,bhkj->bhvj', S, P_c) + D_c, S

    S0 = jnp.zeros((bsz, nh, n, n), f32)
    _, S_in = lax.scan(step, S0, (jnp.moveaxis(P, 1, 0), jnp.moveaxis(D, 1, 0)))
    S_in = jnp.moveaxis(S_in, 0, 1)
    y = Y_intra + jnp.einsum('bnhck,bnhvk->bnhcv', Q_eff, S_in)
    return y.transpose(0, 1, 3, 2, 4).reshape(bsz, seq, nh, n)

def rwkv7_mix(u, mu, w0, w_up, a0, a_up, g_up, k_k, k_a, r_k, gn_g, gn_b):
    f32 = jnp.float32
    u = u + (token_shift(u) - u) * mu
    r, k, v, xw, xa, xg = split_cols(u, RW_SPLITS)
    w_log = -jax.nn.softplus(-(w0 + jnp.tanh(xw) @ w_up)) - 0.5
    log_w = -jnp.exp(w_log.astype(f32))
    a = jax.nn.sigmoid(a0 + xa @ a_up)
    g = jax.nn.sigmoid(xg) @ g_up
    kk = heads(k * k_k, RW_HEADS).astype(f32)
    kk = kk / jnp.maximum(jnp.linalg.norm(kk, axis=-1, keepdims=True), 1e-12)
    k = k * (1 + (a - 1) * k_a)
    r_h, k_h, v_h, a_h = (heads(t, RW_HEADS) for t in (r, k, v, a))
    y = rwkv7_chunked(r_h, heads(log_w, RW_HEADS), k_h, v_h, -kk, kk * a_h.astype(f32))
    y = head_norm(y, gn_g, gn_b, RW_GN_EPS)
    bonus = (jnp.sum(r_h * k_h * r_k, axis=-1, keepdims=True) * v_h).reshape(y.shape)
    return ((y + bonus) * g).astype(u.dtype)

def stick_breaking_attention(q, k, v):
    bsz, seq, nh, hd = q.shape
    f32 = jnp.float32
    qf = (q.astype(f32) * (hd ** -0.5)).transpose(0, 2, 1, 3)
    kf = k.astype(f32).transpose(0, 2, 1, 3)
    vf = v.astype(f32).transpose(0, 2, 1, 3)
    incl_upper = jnp.triu(jnp.ones((SB_BLOCK, SB_BLOCK), f32))
    diag_mask = jnp.tril(jnp.ones((SB_BLOCK, SB_BLOCK), bool), -1)
    outs = []
    for i in range(seq // SB_BLOCK):
        nk = i + 1
        lk = nk * SB_BLOCK
        qb = qf[:, :, i * SB_BLOCK:lk]
        z = jnp.einsum('bhqd,bhkd->bhqk', qb, kf[:, :, :lk]).reshape(bsz, nh, SB_BLOCK, nk, SB_BLOCK)
        mask = jnp.concatenate([jnp.ones((SB_BLOCK, i, SB_BLOCK), bool), diag_mask[:, None, :]], axis=1)
        m = jnp.where(mask, -jax.nn.softplus(z), 0.0)
        within = jnp.einsum('bhqnj,ij->bhqni', m, incl_upper)
        later = jnp.triu(jnp.ones((nk, nk), f32), 1)
        carry = jnp.einsum('bhqm,nm->bhqn', jnp.sum(m, axis=-1), later)
        att = jnp.where(mask, jnp.exp(z + within + carry[..., None]), 0.0)
        vb = vf[:, :, :lk].reshape(bsz, nh, nk, SB_BLOCK, hd)
        outs.append(jnp.einsum('bhqnk,bhnkd->bqhd', att, vb))
    return jnp.concatenate(outs, axis=1).reshape(bsz, seq, nh * hd).astype(q.dtype)

def hgrn2_mix(q_raw, f_raw, i_val, out_gate, lb, norm_g):
    bsz, seq, _ = q_raw.shape
    nc = seq // HG_CHUNK
    f32 = jnp.float32
    q = jax.nn.sigmoid(q_raw.astype(f32))
    log_f = jnp.logaddexp(jnp.log(lb), jnp.log1p(-lb) + jax.nn.log_sigmoid(f_raw.astype(f32)))
    k = -jnp.expm1(log_f)

    def chunks(t, hd):
        return t.reshape(bsz, nc, HG_CHUNK, HG_HEADS, hd).transpose(0, 1, 3, 2, 4)

    q, k, g = chunks(q, HG_EXPAND), chunks(k, HG_EXPAND), chunks(log_f, HG_EXPAND)
    v = chunks(i_val.astype(f32), HG_HEAD_V)
    G = jnp.cumsum(g, axis=3)
    causal = jnp.tril(jnp.ones((HG_CHUNK, HG_CHUNK), bool))[:, :, None]
    diff = jnp.where(causal, G[..., :, None, :] - G[..., None, :, :], -jnp.inf)
    att = jnp.sum(q[..., :, None, :] * jnp.exp(diff) * k[..., None, :, :], axis=-1)
    intra = jnp.einsum('bnhts,bnhsv->bnhtv', att, v)
    G_last = G[..., -1:, :]
    D = jnp.einsum('bnhsk,bnhsv->bnhkv', k * jnp.exp(G_last - G), v)
    gam = jnp.exp(G_last[..., 0, :])

    def step(S, inp):
        gam_c, D_c = inp
        return gam_c[..., None] * S + D_c, S

    S0 = jnp.zeros((bsz, HG_HEADS, HG_EXPAND, HG_HEAD_V), f32)
    _, S_in = lax.scan(step, S0, (jnp.moveaxis(gam, 1, 0), jnp.moveaxis(D, 1, 0)))
    S_in = jnp.moveaxis(S_in, 0, 1)
    inter = jnp.einsum('bnhtk,bnhkv->bnhtv', q * jnp.exp(G), S_in)
    o = (inter + intra).transpose(0, 1, 3, 2, 4).reshape(bsz, seq, HG_HEADS, HG_HEAD_V)
    o = head_rms_norm(o, norm_g, HG_EPS)
    return (o * jax.nn.silu(out_gate.astype(f32))).astype(q_raw.dtype)

def hybrid_mixer(h, w_in, rw_mu, rw_w0, rw_w_up, rw_a0, rw_a_up, rw_g_up, rw_k_k, rw_k_a,
                 rw_r_k, rw_gn_g, rw_gn_b, lb, hg_norm_g, w_br_rw, w_br_sb, w_br_hg, w_out):
    u_rw, u_sb, u_hg, u_gate = split_cols(h @ w_in, IN_SPLITS)
    y_rw = rwkv7_mix(u_rw, rw_mu, rw_w0, rw_w_up, rw_a0, rw_a_up, rw_g_up, rw_k_k, rw_k_a,
                     rw_r_k, rw_gn_g, rw_gn_b)
    q, k, v = (heads(t, SB_HEADS) for t in split_cols(u_sb, [SB_WIDTH] * 3))
    y_sb = stick_breaking_attention(q, k, v)
    hq, hf, hi, hg = split_cols(u_hg, HG_SPLITS)
    y_hg = hgrn2_mix(hq, hf, hi, hg, lb, hg_norm_g)
    g_rw, g_sb, g_hg = split_cols(jax.nn.sigmoid(u_gate), [D_MODEL] * N_BRANCH)
    merged = g_rw * (y_rw @ w_br_rw) + g_sb * (y_sb @ w_br_sb) + g_hg * (y_hg @ w_br_hg)
    return merged @ w_out

def setup_inputs(seed: int = 0) -> dict:
    key = jax.random.key(seed)
    ks = jax.random.split(key, 32)
    L = DEPTH
    D = D_MODEL

    def nrm(k, shape, scale):
        return jax.random.normal(k, shape, jnp.float32) * scale

    return {
        "x": nrm(ks[0], (BATCH, SEQ, D), 1.0),
        "p": nrm(ks[1], (L, BATCH, SEQ, PLE_DIM), 1.0),
        "ln_g": 1.0 + nrm(ks[2], (L, 4, D), 0.02),
        "ln_b": nrm(ks[3], (L, 4, D), 0.01),
        "ffn1_wg": nrm(ks[4], (L, D, D_FF), D ** -0.5),
        "ffn1_wu": nrm(ks[5], (L, D, D_FF), D ** -0.5),
        "ffn1_wd": nrm(ks[6], (L, D_FF, D), BETA * D_FF ** -0.5),
        "w_in": nrm(ks[7], (L, D, IN_COLS), D ** -0.5),
        "rw_mu": jax.random.uniform(ks[8], (L, RW_COLS), jnp.float32, 0.05, 0.95),
        "rw_w0": jax.random.uniform(ks[9], (L, RW_WIDTH), jnp.float32, -6.0, -1.0),
        "rw_w_up": nrm(ks[10], (L, RW_DECAY_LORA, RW_WIDTH), 0.1 * RW_DECAY_LORA ** -0.5),
        "rw_a0": nrm(ks[11], (L, RW_WIDTH), 0.1),
        "rw_a_up": nrm(ks[12], (L, RW_AAA_LORA, RW_WIDTH), 0.1 * RW_AAA_LORA ** -0.5),
        "rw_g_up": nrm(ks[13], (L, RW_GATE_LORA, RW_WIDTH), RW_GATE_LORA ** -0.5),
        "rw_k_k": 0.85 + nrm(ks[14], (L, RW_WIDTH), 0.05),
        "rw_k_a": 1.0 + nrm(ks[15], (L, RW_WIDTH), 0.05),
        "rw_r_k": nrm(ks[16], (L, RW_HEADS, RW_HEAD_DIM), 0.1),
        "rw_gn_g": 1.0 + nrm(ks[17], (L, RW_WIDTH), 0.02),
        "rw_gn_b": nrm(ks[18], (L, RW_WIDTH), 0.01),
        "hg_lb_raw": nrm(ks[19], (L, HG_FWIDTH), 0.1),
        "hg_norm_g": 1.0 + nrm(ks[20], (L, HG_VWIDTH), 0.02),
        "w_br_rw": nrm(ks[21], (L, RW_WIDTH, D), RW_WIDTH ** -0.5),
        "w_br_sb": nrm(ks[22], (L, SB_WIDTH, D), SB_WIDTH ** -0.5),
        "w_br_hg": nrm(ks[23], (L, HG_VWIDTH, D), HG_VWIDTH ** -0.5),
        "w_out": nrm(ks[24], (L, D, D), BETA * D ** -0.5),
        "ffn2_wg": nrm(ks[25], (L, D, D_FF), D ** -0.5),
        "ffn2_wu": nrm(ks[26], (L, D, D_FF), D ** -0.5),
        "ffn2_wd": nrm(ks[27], (L, D_FF, D), BETA * D_FF ** -0.5),
        "ple_gate": nrm(ks[28], (L, D, D), D ** -0.5),
        "ple_proj": nrm(ks[29], (L, PLE_DIM, D), BETA * PLE_DIM ** -0.5),
    }

def reference(x, p, ln_g, ln_b, ffn1_wg, ffn1_wu, ffn1_wd, w_in, rw_mu, rw_w0, rw_w_up, rw_a0,
              rw_a_up, rw_g_up, rw_k_k, rw_k_a, rw_r_k, rw_gn_g, rw_gn_b, hg_lb_raw, hg_norm_g,
              w_br_rw, w_br_sb, w_br_hg, w_out, ffn2_wg, ffn2_wu, ffn2_wd, ple_gate, ple_proj):
    lb_sm = jax.nn.softmax(hg_lb_raw.astype(jnp.float32), axis=0)
    lb_all = jnp.cumsum(lb_sm, axis=0)
    lb_all = lb_all - lb_all[0:1]
    h = x
    for i in range(DEPTH):
        h = layer_norm(ALPHA * h + 0.5 * swiglu(h, ffn1_wg[i], ffn1_wu[i], ffn1_wd[i]), ln_g[i, 0], ln_b[i, 0])
        mix = hybrid_mixer(h, w_in[i], rw_mu[i], rw_w0[i], rw_w_up[i], rw_a0[i], rw_a_up[i], rw_g_up[i],
                           rw_k_k[i], rw_k_a[i], rw_r_k[i], rw_gn_g[i], rw_gn_b[i], lb_all[i],
                           hg_norm_g[i], w_br_rw[i], w_br_sb[i], w_br_hg[i], w_out[i])
        h = layer_norm(ALPHA * h + mix, ln_g[i, 1], ln_b[i, 1])
        h = layer_norm(ALPHA * h + 0.5 * swiglu(h, ffn2_wg[i], ffn2_wu[i], ffn2_wd[i]), ln_g[i, 2], ln_b[i, 2])
        ple = jax.nn.sigmoid(h @ ple_gate[i]) * (p[i] @ ple_proj[i])
        h = layer_norm(ALPHA * h + ple, ln_g[i, 3], ln_b[i, 3])
    return h


_drawn_inputs = setup_inputs


def setup_inputs(seed=0):
    import zlib

    import numpy as np

    out = dict(_drawn_inputs(seed))
    spreads = {}
    factors = {'rw_w_up': 8.0,
     'rw_a0': 8.0,
     'rw_a_up': 8.0,
     'rw_k_k': 8.0,
     'rw_k_a': 7.196,
     'rw_gn_g': 24.746,
     'rw_gn_b': 39.377,
     'hg_lb_raw': 29.019,
     'hg_norm_g': 23.868}
    for name, (base, spread) in spreads.items():
        noise = np.random.default_rng([zlib.crc32(name.encode()), seed]).standard_normal(out[name].shape)
        drawn = base * np.exp(spread * noise) if base else spread * noise
        out[name] = jnp.asarray(drawn.astype(out[name].dtype))
    for name, factor in factors.items():
        out[name] = (out[name] * factor).astype(out[name].dtype)
    return out
```

```python
from contextlib import ExitStack

import numpy as np

import concourse.bass as bass
from concourse import mybir

F32 = mybir.dt.float32
F32R = mybir.dt.float32r
I32 = mybir.dt.int32
ALU = mybir.AluOpType
ACT = mybir.ActivationFunctionType
AX = mybir.AxisListType

P = 128
D = 1024
SEQ = 512
DEPTH = 2
PLE = 256
FF = 2816
KD = D // P
NT = SEQ // P
FT = FF // P
ALPHA = (2 * DEPTH) ** 0.25
LN_EPS = 1e-5
GN_EPS = 64e-5
HG_EPS = 1e-5
HEAD = 64
NC = SEQ // HEAD
DECAY = float(np.exp(-0.5))
LOG_ZERO = -1e30
SS_SCALE = float(2.0 ** 20)

C_R, C_K, C_V, C_W, C_XG = 0, 512, 1024, 1536, 1664
C_SB = 1824
C_HG = C_SB + 1536
C_GATE = C_HG + 2048

K_ID, K_NTRI, K_NONE, K_ONES64, K_CAUSAL, K_RW, K_RX, K_HG = 0, 1, 2, 3, 4, 5, 7, 13
RX_LEVELS = [1, 2, 4, 8, 16, 32]
HG_LEVELS = [1, 2, 4, 8, 16, 32, 64]
N_CONST = K_HG + len(HG_LEVELS)

R_LNG, R_LNB, R_MU, R_W0, R_A0, R_KK, R_KA, R_RK, R_LB = 0, 32, 64, 79, 83, 87, 91, 95, 99

RAW_RING = 4
SPLIT_RING = 3


def constants():
    i = np.arange(P)[:, None]
    j = np.arange(P)[None, :]
    blocks = [i == j, -1.0 * (i >= j), -np.ones((P, P)), i // 64 == j // 64, i < j,
              (i // 64 == j // 64) & (i < j), (i // 64 == j // 64) & (i <= j)]
    pair = lambda late, early, h: (late // (2 * h) == early // (2 * h)) & (late // h % 2 == 1) & (early // h % 2 == 0)
    blocks += [pair(i, j, h) for h in RX_LEVELS]
    blocks += [pair(j, i, h) for h in HG_LEVELS]
    return np.concatenate([np.asarray(b, np.float32) for b in blocks], axis=1)


def dense_groups(a):
    groups = []

    def add(name, pieces, rows, widths):
        slots = []
        for s in range(rows // 256):
            slots.append([(w[s * 256:(s + 1) * 256, c:c + n].rearrange("(k p) n -> p k n", p=P), at, n)
                          for w, c, at, n in pieces])
        groups.append((name, slots, widths))

    four = [P] * 4
    for L in range(DEPTH):
        for f in range(2):
            wg, wu, wd = ((a["ffn1_wg"], a["ffn1_wu"], a["ffn1_wd"]), (a["ffn2_wg"], a["ffn2_wu"], a["ffn2_wd"]))[f]
            if f == 1:
                w_in = a["w_in"][L]

                def cols(name, c):
                    add(name, [(w_in, c, 0, 512)], D, four)

                for n in range(3):
                    cols(("sb", L, n), C_SB + 512 * n)
                for n in range(4):
                    cols(("hg", L, n), C_HG + 512 * n)
                add(("lora", L), [(w_in, C_W, 0, 288)], D, [P, P, 32])
                for ft in range(4):
                    add(("rkv", L, ft), [(w_in, c + P * ft, P * n, P) for n, c in enumerate((C_R, C_K, C_V))],
                        D, [P] * 3)
                for half in range(2):
                    for br, (key, col) in enumerate((("w_br_sb", 1), ("w_br_hg", 2), ("w_br_rw", 0))):
                        cols(("gate", L, half, br), C_GATE + D * col + 512 * half)
                        add(("branch", L, half, br), [(a[key][L], 512 * half, 0, 512)], 512, four)
                for half in range(2):
                    add(("out", L, half), [(a["w_out"][L], 512 * half, 0, 512)], D, four)
            for g in range(FT // 2):
                add(("up", L, f, g), [(wg[L], 256 * g, 0, 256), (wu[L], 256 * g, 256, 256)], D, four)
            for half in range(2):
                add(("down", L, f, half), [(wd[L], 512 * half, 0, 512)], FF, four)
        for half in range(2):
            add(("pgate", L, half), [(a["ple_gate"][L], 512 * half, 0, 512)], D, four)
            add(("pproj", L, half), [(a["ple_proj"][L], 512 * half, 0, 512)], PLE, four)
    return groups


def build(nc, a, out, counts, banks_of):
    ctx = ExitStack()
    with ctx:
        sems, reached = {}, {}

        def sem_of(name):
            if name not in sems:
                sems[name] = ctx.enter_context(nc.semaphore(name))
                reached[name] = 0
            return sems[name]

        def step(name, *index, by=1):
            s = sem_of(name)
            reached[name] += by
            counts[(name, *index)] = reached[name]
            return s, by

        def after(name, *index):
            return sem_of(name), counts.get((name, *index), 1)

        def sb(stack, name, shape, dt=F32):
            return stack.enter_context(nc.sbuf_tensor(name, shape, dt))

        cons = sb(ctx, "cons", [P, N_CONST, P])
        hT = [sb(ctx, "hT_hi", [P, KD, SEQ], F32R), sb(ctx, "hT_lo", [P, KD, SEQ], F32R)]
        w_raw = sb(ctx, "w_raw", [P, RAW_RING, 2, 512])
        w_split = [sb(ctx, "w_hi", [P, SPLIT_RING, 2, 512], F32R), sb(ctx, "w_lo", [P, SPLIT_RING, 2, 512], F32R)]
        zero = sb(ctx, "zero", [P, 1])
        par = sb(ctx, "par", [P, P])
        parT = sb(ctx, "parT", [P, P])
        lbT = sb(ctx, "lbT", [P, 24])
        ln_small = sb(ctx, "ln_small", [P, NT, 16])
        ln_mv = sb(ctx, "ln_mv", [P, NT, 2])
        ln_rstd = sb(ctx, "ln_rstd", [P, NT, 1])

        ps = [ctx.enter_context(nc.psum_tensor(f"ps{b}", [P, 512], F32)) for b in range(8)]

        def ident():
            return cons[:, K_ID, :]

        with ExitStack() as own:
            h_tok = sb(own, "h_tok", [P, NT, D])
            with ExitStack() as o2:
                aT = [sb(o2, "aT_hi", [P, FT, SEQ], F32R), sb(o2, "aT_lo", [P, FT, SEQ], F32R)]
                silu = sb(o2, "silu", [P, 2, SEQ])
                act_raw = sb(o2, "act_raw", [P, 2, SEQ])
            with ExitStack() as o2:
                ln_rows = sb(o2, "ln_rows", [P, 2, D])
                h_raw = sb(o2, "h_raw", [P, 2, SEQ])
                h_new = sb(o2, "h_new", [P, 2, D])
                p_tok = sb(o2, "p_tok", [P, NT, PLE])
                p_raw = sb(o2, "p_raw", [P, 2, SEQ])
                pT = [sb(o2, "pT_hi", [P, 2, SEQ], F32R), sb(o2, "pT_lo", [P, 2, SEQ], F32R)]
                ple_sig = sb(o2, "ple_sig", [P, 4, 512])
                ple_pr = sb(o2, "ple_pr", [P, 512])
        with ExitStack() as own:
            y_raw = sb(own, "y_raw", [P, 3, 4, SEQ])
            with ExitStack() as o2:
                sb_q = sb(o2, "sb_q", [P, 4, SEQ])
                sb_k = sb(o2, "sb_k", [P, 4, SEQ])
                sb_v = sb(o2, "sb_v", [P, NT, 512])
                sb_e = sb(o2, "sb_e", [P, 2, SEQ])
                sb_sp = sb(o2, "sb_sp", [P, 4, SEQ])
                sb_att = sb(o2, "sb_att", [P, 4, SEQ])
            with ExitStack() as o2:
                hg_q = sb(o2, "hg_q", [P, 4, SEQ])
                hg_k = sb(o2, "hg_k", [P, 4, SEQ])
                hg_p = sb(o2, "hg_p", [P, 4, SEQ])
                hg_x = sb(o2, "hg_x", [P, 4, SEQ])
                hg_v = sb(o2, "hg_v", [P, NT, 512])
                hg_g = sb(o2, "hg_g", [P, NT, 512])
                hg_Q = sb(o2, "hg_Q", [P, 4, SEQ])
                hg_K = sb(o2, "hg_K", [P, 4, SEQ])
                hg_e = sb(o2, "hg_e", [P, 2, 1024])
                hg_att = sb(o2, "hg_att", [P, NT, 4, P])
                hg_S = sb(o2, "hg_S", [P, NT, 4, P])
                hg_row = sb(o2, "hg_row", [P, 512])
            with ExitStack() as o2:
                rw_u = sb(o2, "rw_u", [P, 3, SEQ + 1])
                rw_d = sb(o2, "rw_d", [P, SEQ])
                rkv = sb(o2, "rkv", [P, 3, SEQ])
                lora_x = sb(o2, "lora_x", [P, 3, SEQ])
                w_up = sb(o2, "w_up", [P, 512])
                g_up = sb(o2, "g_up", [P, 2, 512])
                gn_rows = sb(o2, "gn_rows", [P, 2, 512])
                rw_sw = sb(o2, "rw_sw", [P, SEQ])
                rw_a = sb(o2, "rw_a", [P, SEQ])
                rw_cs = sb(o2, "rw_cs", [P, SEQ])
                rw_e3 = sb(o2, "rw_e3", [P, SEQ])
                rw_e1 = sb(o2, "rw_e1", [P, SEQ])
                rw_kk = sb(o2, "rw_kk", [P, SEQ])
                rw_ss = sb(o2, "rw_ss", [P, SEQ])
                rw_k2 = sb(o2, "rw_k2", [P, SEQ])
                rw_b = sb(o2, "rw_b", [P, SEQ])
                rw_dec = sb(o2, "rw_dec", [P, 2, SEQ])
                rw_keep = sb(o2, "rw_keep", [P, SEQ])
                ar = sb(o2, "ar", [P, NT, 2, P])
                b_inv = sb(o2, "b_inv", [P, SEQ])
                k_inv = sb(o2, "k_inv", [P, SEQ])
                b_tok = sb(o2, "b_tok", [P, NT, P])
                k_tok = sb(o2, "k_tok", [P, NT, P])
                v_tok = sb(o2, "v_tok", [P, NT, P])
                rhs = sb(o2, "rhs", [P, 2, NT, P])
                bm = sb(o2, "bm", [P, 2, NT, 2, P])
                km = sb(o2, "km", [P, 2, NT, 2, P])
                inv = sb(o2, "inv", [P, 2, NT, P])
                invT = sb(o2, "invT", [P, 2, NT, P])
                xx = sb(o2, "xx", [P, 2, NT, P])
                s_pre = sb(o2, "s_pre", [P, HEAD])
                bonus = sb(o2, "bonus", [P, NT, 2])
                rk_sel = sb(o2, "rk_sel", [P, 4, 2])
                gn_st = sb(o2, "gn_st", [P, 2, NT, 2])
            rw_bd, rw_kd = rw_dec[:, 0, :], rw_dec[:, 1, :]
            yt = rw_dec[:, :, :].rearrange("p a (t n) -> p a t n", n=P)
            q_eff = inv[:, 0, :, :].rearrange("p t n -> p (t n)")
            p_mat = inv[:, 1, :, :].rearrange("p t (c n) -> p (t c) n", c=2)
            d_mat = rhs[:, 0, :, :].rearrange("p t (c n) -> p (t c) n", c=2)
            s_all = rhs[:, 1, :, :].rearrange("p t (c n) -> p (t c) n", c=2)
            with ExitStack() as o2:
                yT = [sb(o2, "yT_hi", [P, 4, SEQ], F32R), sb(o2, "yT_lo", [P, 4, SEQ], F32R)]
                gate_s = sb(o2, "gate_s", [P, 4, SEQ])
                m_tmp = sb(o2, "m_tmp", [P, SEQ])
                m_acc = sb(o2, "m_acc", [P, KD, SEQ])
                mT = [sb(o2, "mT_hi", [P, KD, SEQ], F32R), sb(o2, "mT_lo", [P, KD, SEQ], F32R)]
        h_dram = nc.dram_tensor("h_dram", (NT, P, D), F32).ap()

        groups = dense_groups(a)
        slot_list = [(pieces, g, i) for g in groups for i, pieces in enumerate(g[1])]
        slot_free = {}

        block = ctx.enter_context(nc.Block())

        def hg_o_buf(t):
            return hg_x[:, t, :]

        def unit(hd):
            return slice(HEAD * hd, HEAD * hd + HEAD)

        def rwkv_set_pe(pe, take, L, ft):
            if ft == 0:
                pe.wait_ge(*after("lora_act", L))
                pe.wait_ge(*after("rw_wts", L))
            b = take(("rww", L, ft), ("rw_sw", L, ft))
            nc.tensor.matmul(b[:, :], w_up[0:64, ft * P:(ft + 1) * P], lora_x[0:64, 0, :], start=True,
                             stop=True).then_inc(*step("rww_done", L, ft))
            b = take(("rwa", L, ft), ("rw_a", L, ft))
            nc.tensor.matmul(b[:, :], w_up[64:128, ft * P:(ft + 1) * P], lora_x[64:128, 0, :], start=True,
                             stop=True).then_inc(*step("rwa_done", L, ft))
            pe.wait_ge(*after("rw_sq", L, ft))
            b = take(("rwss", L, ft), ("rw_ssmax", L, ft))
            nc.tensor.matmul(b[:, :], cons[:, K_ONES64, :], rw_ss[:, :], start=True,
                             stop=True).then_inc(*step("rwss_done", L, ft))
            pe.wait_ge(*after("rkv_mix", L, ft, 2))
            pe.wait_ge(*after("rw_kd", L, ft))
            for i, src in enumerate((rkv[:, 2, :], None, rw_bd[:, :], rw_kd[:, :])):
                b = take(("rwt", L, ft, i), ("rw_tok", L, ft, i))
                for t in range(NT):
                    s_ = ar[:, t, 0, :] if src is None else src[:, t * P:(t + 1) * P]
                    ins = nc.tensor.transpose(b[:, t * P:(t + 1) * P], s_, ident())
                ins.then_inc(*step("rwt_done", L, ft, i))
            for i, src in enumerate((b_inv, k_inv)):
                for hd in range(2):
                    for tp in range(2):
                        b = take(("rwm", L, ft, i, hd, tp), ("rw_mask", L, ft, i, hd, tp))
                        for t in (2 * tp, 2 * tp + 1):
                            ins = nc.tensor.matmul(b[:, (t % 2) * 256:(t % 2) * 256 + 256], src[unit(hd), t * P:(t + 1) * P],
                                                   ar[unit(hd), t, :, :].rearrange("p a n -> p (a n)"), start=True, stop=True)
                        ins.then_inc(*step("rwm_done", L, ft, i, hd, tp))
            b = take(("rwb", L, ft), ("rw_bonus", L, ft))
            pe.wait_ge(*after("rw_rk", L, ft))
            for t in range(NT):
                ins = nc.tensor.matmul(b[:, 2 * t:2 * t + 2], rw_keep[:, t * P:(t + 1) * P], rk_sel[:, ft, :], start=True, stop=True)
            ins.then_inc(*step("rwb_done", L, ft))
            for lev in range(len(RX_LEVELS)):
                for hd in range(2):
                    b = take(("rwx", L, ft, lev, hd), ("rw_x", L, ft, lev, hd))
                    if lev == 0:
                        for tp in range(2):
                            pe.wait_ge(*after("rw_mask", L, ft, 0, hd, tp))
                    else:
                        pe.wait_ge(*after("rw_inv", L, ft, lev - 1, hd))
                        pe.wait_ge(*after("rw_invT", L, ft, lev - 1, hd))
                    for t in range(NT):
                        ins = nc.tensor.matmul(b[:, t * P:(t + 1) * P], bm[:, hd, t, 0, :],
                                               ident() if lev == 0 else inv[:, hd, t, :], start=True, stop=True)
                    ins.then_inc(*step("rwx_done", L, ft, lev, hd))
                if lev == 0:
                    continue
                for hd in range(2):
                    pe.wait_ge(*after("rw_x", L, ft, lev, hd))
                    if lev < len(RX_LEVELS) - 1:
                        b = take(("rwi", L, ft, lev, hd), ("rw_inv", L, ft, lev, hd))
                        for t in range(NT):
                            ins = nc.tensor.matmul(b[:, t * P:(t + 1) * P], invT[:, hd, t, :], xx[:, hd, t, :], start=True, stop=True)
                        ins.then_inc(*step("rwi_done", L, ft, lev, hd))
                    b = take(("rwj", L, ft, lev, hd), ("rw_invT", L, ft, lev, hd))
                    for t in range(NT):
                        ins = nc.tensor.matmul(b[:, t * P:(t + 1) * P], xx[:, hd, t, :], invT[:, hd, t, :], start=True, stop=True)
                    ins.then_inc(*step("rwj_done", L, ft, lev, hd))
            for hd in range(2):
                for tp in range(2):
                    pe.wait_ge(*after("rw_mask", L, ft, 1, hd, tp))
            pe.wait_ge(*after("rw_tok", L, ft, 0))
            b = take(("rwl", L, ft), ("rw_lakv", L, ft))
            for hd in range(2):
                for t in range(NT):
                    c = (hd * NT + t) * HEAD
                    ins = nc.tensor.matmul(b[:, c:c + HEAD], km[:, hd, t, 0, :], v_tok[:, t, unit(hd)], start=True, stop=True)
            ins.then_inc(*step("rwl_done", L, ft))
            pe.wait_ge(*after("rw_lakv", L, ft))
            pe.wait_ge(*after("rw_tok", L, ft, 1))
            for hd in range(2):
                b = take(("rwu", L, ft, hd), ("rw_wu", L, ft, hd))
                pe.wait_ge(*after("rw_invT", L, ft, len(RX_LEVELS) - 1, hd))
                for t in range(NT):
                    ins = nc.tensor.matmul(b[:, t * P:(t + 1) * P], invT[:, hd, t, :], rhs[:, hd, t, :], start=True, stop=True)
                ins.then_inc(*step("rwu_done", L, ft, hd))
            for hd in range(2):
                pe.wait_ge(*after("rw_wu", L, ft, hd))
            pe.wait_ge(*after("rw_tok", L, ft, 3))
            for cp in range(2):
                b = take(("rwp", L, ft, cp), ("rw_p", L, ft, cp))
                cs = slice(HEAD * cp, HEAD * cp + HEAD)
                for hd in range(2):
                    for t in range(NT):
                        ins = nc.tensor.matmul(b[unit(hd), t * HEAD:(t + 1) * HEAD], xx[cs, hd, t, 0:HEAD], b_tok[cs, t, unit(hd)],
                                               start=True, stop=True)
                ins.then_inc(*step("rwp_done", L, ft, cp))
            for cp in range(2):
                b = take(("rwd", L, ft, cp), ("rw_d", L, ft, cp))
                cs = slice(HEAD * cp, HEAD * cp + HEAD)
                for hd in range(2):
                    for t in range(NT):
                        nc.tensor.matmul(b[unit(hd), t * HEAD:(t + 1) * HEAD], b_tok[cs, t, unit(hd)], xx[cs, hd, t, HEAD:P],
                                         start=True, stop=False)
                        ins = nc.tensor.matmul(b[unit(hd), t * HEAD:(t + 1) * HEAD], k_tok[cs, t, unit(hd)], v_tok[cs, t, unit(hd)],
                                               start=False, stop=True)
                ins.then_inc(*step("rwd_done", L, ft, cp))
            b = take(("rwq", L, ft), ("rw_q", L, ft))
            for hd in range(2):
                for t in range(NT):
                    ins = nc.tensor.matmul(b[unit(hd), t * P:(t + 1) * P], xx[:, hd, t, 0:HEAD], bm[:, hd, t, 1, :],
                                           start=True, stop=True)
            ins.then_inc(*step("rwq_done", L, ft))
            pe.wait_ge(*after("rw_p", L, ft, 1))
            for c in range(1, NC - 1):
                b = take(("rws", L, ft, c), ("rw_state", L, ft, c))
                pe.wait_ge(*after("rw_state", L, ft, c - 1))
                for hd in range(2):
                    ins = nc.tensor.matmul(b[unit(hd), 0:HEAD], p_mat[unit(hd), c, :], s_all[unit(hd), c, :], start=True, stop=True)
                ins.then_inc(*step("rws_done", L, ft, c))
            pe.wait_ge(*after("rw_q", L, ft))
            pe.wait_ge(*after("rw_state", L, ft, NC - 2))
            for hd in range(2):
                b = take(("rwy", L, ft, hd), ("rw_y2", L, ft, hd))
                for t in range(NT):
                    c0 = t * HEAD
                    nc.tensor.matmul(b[:, c0:c0 + HEAD], bm[:, hd, t, 1, :], xx[:, hd, t, HEAD:P], start=True, stop=False,
                                     skip_group_check=True)
                    ins = nc.tensor.matmul(b[:, c0:c0 + HEAD], km[:, hd, t, 1, :], v_tok[:, t, unit(hd)], start=False,
                                           stop=False, skip_group_check=True)
                    for cp in range(2):
                        c = 2 * t + cp
                        if c == 0:
                            continue
                        ins = nc.tensor.matmul(b[HEAD * cp:HEAD * cp + HEAD, c0:c0 + HEAD], q_eff[unit(hd), c * HEAD:(c + 1) * HEAD],
                                               s_all[unit(hd), c, :], start=False, stop=cp == 1, skip_group_check=True)
                ins.then_inc(*step("rwy_done", L, ft, hd))
            b = take(("rwg", L, ft), ("rw_gated", L, ft))
            for t in range(NT):
                nc.tensor.matmul(b[:, t * P:(t + 1) * P], lora_x[:, 1, t * P:(t + 1) * P], g_up[:, 0, ft * P:(ft + 1) * P],
                                 start=True, stop=False)
                ins = nc.tensor.matmul(b[:, t * P:(t + 1) * P], lora_x[0:32, 2, t * P:(t + 1) * P],
                                       g_up[0:32, 1, ft * P:(ft + 1) * P], start=False, stop=True)
            ins.then_inc(*step("rwg_done", L, ft))
            pe.wait_ge(*after("rw_gated", L, ft))
            b = take(("rwo", L, ft), ("rw_yT", L, ft))
            for t in range(NT):
                ins = nc.tensor.transpose(b[:, t * P:(t + 1) * P], yt[:, 0, t, :], ident())
            ins.then_inc(*step("rwo_done", L, ft))

        def gn_small(which):
            return ln_small[:, :, 0:4]

        def shift_mix(v, chain, u, d, dst, mu):
            chain(v.tensor_tensor(d, u[:, 0:SEQ], u[:, 1:SEQ + 1], ALU.subtract))
            return v.scalar_tensor_tensor(dst, d, mu, u[:, 1:SEQ + 1], ALU.mult, ALU.add)

        def rwkv_set_dve(v, now, chain, L, ft):
            if ft:
                now("rwt_done", L, ft - 1, 3)
                now("rwb_done", L, ft - 1)
            for m in range(3):
                now("rkv_in", L, ft, m)
                if m:
                    now("rkv_mix", L, ft, m - 1)
                col = R_MU + 4 * m + ft
                shift_mix(v, chain, rw_u[:, m, :], rw_d[:, :], rkv[:, m, :], parT[:, col:col + 1]).then_inc(*step("rkv_mix", L, ft, m))
            now("rkv_mix", L, ft, 2)
            v.tensor_scalar(rw_kk[:, :], rkv[:, 1, :], parT[:, R_KK + ft:R_KK + ft + 1], None, ALU.mult).then_inc(*step("rw_kkr", L, ft))
            now("rw_sw", L, ft)
            chain(v.memset(rw_e1[:, :], 1.0))
            chain(v.memset(rw_e1[:, :].rearrange("p (c n) -> p c n", n=HEAD)[:, :, 0:1], 0.0))
            chain(v.tensor_tensor_scan(rw_cs[:, :], rw_e1[:, :], rw_sw[:, :], 0.0, ALU.mult, ALU.add))
            v.tensor_tensor(rw_e3[:, :], rw_cs[:, :], rw_sw[:, :], ALU.subtract).then_inc(*step("rw_csm", L, ft))
            now("rwss_done", L, ft)
            v.tensor_scalar(rw_ss[:, :], ps[banks_of.get(("rwss", L, ft), 0)][:, :], 1e-24, None, ALU.max).then_inc(*step("rw_ssmax", L, ft))
            now("rw_a", L, ft)
            chain(v.tensor_scalar(rw_k2[:, :], rw_a[:, :], 1.0, parT[:, R_KA + ft:R_KA + ft + 1], ALU.subtract, ALU.mult))
            chain(v.scalar_tensor_tensor(rw_k2[:, :], rw_k2[:, :], 1.0, rkv[:, 1, :], ALU.add, ALU.mult))
            v.tensor_tensor(rw_keep[:, :], rkv[:, 0, :], rw_k2[:, :], ALU.mult).then_inc(*step("rw_rk", L, ft))
            now("rw_rn", L, ft)
            chain(v.scalar_tensor_tensor(rw_kk[:, :], rw_kk[:, :], SS_SCALE ** 0.5, rw_ss[:, :], ALU.mult, ALU.mult))
            v.tensor_tensor(rw_b[:, :], rw_kk[:, :], rw_a[:, :], ALU.mult).then_inc(*step("rw_b_", L, ft))
            now("rw_b_", L, ft)
            now("rw_e3", L, ft)
            tiles = lambda x: x[:, :].rearrange("p (t n) -> p t n", n=P)
            v.scalar_tensor_tensor(ar[:, :, 0, :], tiles(rw_kk), -1.0, tiles(rw_e3), ALU.mult, ALU.mult)
            v.tensor_tensor(ar[:, :, 1, :], rkv[:, 0, :].rearrange("p (t n) -> p t n", n=P), tiles(rw_e1), ALU.mult)
            chain(v.tensor_tensor(b_inv[:, :], rw_b[:, :], rw_cs[:, :], ALU.mult))
            chain(v.tensor_tensor(k_inv[:, :], rw_k2[:, :], rw_cs[:, :], ALU.mult))
            chunk = lambda x: x[:, :].rearrange("p (c n) -> p c n", n=HEAD)
            last = chunk(rw_e1)[:, :, HEAD - 1:HEAD].to_broadcast([P, NC, HEAD])
            if ft:
                now("rwo_done", L, ft - 1)
            v.tensor_tensor(chunk(rw_bd), chunk(b_inv), last, ALU.mult)
            v.tensor_tensor(chunk(rw_kd), chunk(k_inv), last, ALU.mult).then_inc(*step("rw_kd", L, ft))
            for i, dst in enumerate((bm, km)):
                for hd in range(2):
                    for tp in range(2):
                        now("rwm_done", L, ft, i, hd, tp)
                        b = ps[banks_of.get(("rwm", L, ft, i, hd, tp), 0)]
                        mask = cons[:, K_RW:K_RW + 2, :].rearrange("p a n -> p (a n)")
                        v.tensor_tensor(dst[:, hd, 2 * tp:2 * tp + 2, :, :].rearrange("p t a n -> p t (a n)"),
                                        b[:, :].rearrange("p (t n) -> p t n", t=2), mask.unsqueeze(1).to_broadcast([P, 2, 256]),
                                        ALU.mult).then_inc(*step("rw_mask", L, ft, i, hd, tp))
            now("rwb_done", L, ft)
            v.tensor_copy(bonus[:, :, :], ps[banks_of.get(("rwb", L, ft), 0)][:, 0:8].rearrange("p (t d) -> p t d", d=2)).then_inc(
                *step("rw_bonus", L, ft))
            four = lambda m_: m_.unsqueeze(1).to_broadcast([P, NT, P])
            for lev in range(len(RX_LEVELS)):
                for hd in range(2):
                    now("rwx_done", L, ft, lev, hd)
                    b = ps[banks_of.get(("rwx", L, ft, lev, hd), 0)]
                    v.tensor_tensor(xx[:, hd, :, :], b[:, :].rearrange("p (t n) -> p t n", t=NT), four(cons[:, K_RX + lev, :]),
                                    ALU.mult).then_inc(*step("rw_x", L, ft, lev, hd))
                    if lev == 0:
                        now("rw_x", L, ft, lev, hd)
                        v.tensor_tensor(inv[:, hd, :, :], xx[:, hd, :, :], four(ident()), ALU.add).then_inc(*step("rw_inv", L, ft, 0, hd))
                        chain(v.tensor_tensor(invT[:, hd, :, :], bm[:, hd, :, 0, :], four(cons[:, K_HG, :]), ALU.mult))
                        v.tensor_tensor(invT[:, hd, :, :], invT[:, hd, :, :], four(ident()), ALU.add).then_inc(*step("rw_invT", L, ft, 0, hd))
                if lev == 0:
                    continue
                for hd in range(2):
                    if lev < len(RX_LEVELS) - 1:
                        now("rwi_done", L, ft, lev, hd)
                        now("rw_inv", L, ft, lev - 1, hd)
                        b = ps[banks_of.get(("rwi", L, ft, lev, hd), 0)]
                        v.tensor_tensor(inv[:, hd, :, :], inv[:, hd, :, :], b[:, :].rearrange("p (t n) -> p t n", t=NT),
                                        ALU.add).then_inc(*step("rw_inv", L, ft, lev, hd))
                    now("rwj_done", L, ft, lev, hd)
                    now("rw_invT", L, ft, lev - 1, hd)
                    b = ps[banks_of.get(("rwj", L, ft, lev, hd), 0)]
                    v.tensor_tensor(invT[:, hd, :, :], invT[:, hd, :, :], b[:, :].rearrange("p (t n) -> p t n", t=NT),
                                    ALU.add).then_inc(*step("rw_invT", L, ft, lev, hd))
            now("rwq_done", L, ft)
            v.tensor_tensor(tiles(q_eff), ps[banks_of.get(("rwq", L, ft), 0)][:, :].rearrange("p (t n) -> p t n", n=P), ar[:, :, 1, :],
                            ALU.add).then_inc(*step("rw_q", L, ft))
            now("rw_d", L, ft, 1)
            for c in range(NC - 1):
                if c == 0:
                    v.tensor_copy(s_all[:, 1, :], d_mat[:, 0, :]).then_inc(*step("rw_state", L, ft, c))
                else:
                    chain(v.scalar_tensor_tensor(s_pre[:, :], s_all[:, c, :], rw_e1[:, c * HEAD + HEAD - 1:(c + 1) * HEAD],
                                                 d_mat[:, c, :], ALU.mult, ALU.add))
                    now("rws_done", L, ft, c)
                    v.tensor_tensor(s_all[:, c + 1, :], s_pre[:, :], ps[banks_of.get(("rws", L, ft, c), 0)][:, 0:HEAD],
                                    ALU.add).then_inc(*step("rw_state", L, ft, c))
                now("rw_state", L, ft, c)
            th = lambda x: x.rearrange("p t (d n) -> p (t d) n", d=2)
            y0, y1 = th(yt[:, 0, :, :]), th(yt[:, 1, :, :])
            st = lambda i: gn_st[:, i, :, :].rearrange("p t d -> p (t d)")
            wide = lambda x: x.unsqueeze(2).to_broadcast([P, 2 * NT, HEAD])
            bh = [ps[banks_of.get(("rwy", L, ft, hd), 0)][:, 0:256].rearrange("p (t n) -> p t n", n=HEAD) for hd in range(2)]
            for hd in range(2):
                now("rwy_done", L, ft, hd)
                chain(v.tensor_reduce(gn_st[:, 0, :, hd], bh[hd], AX.X, ALU.add))
            chain(v.tensor_scalar(st(0), st(0), 1.0 / HEAD, None, ALU.mult))
            for hd in range(2):
                v.tensor_tensor(yt[:, 0, :, unit(hd)], bh[hd], gn_st[:, 0, :, hd:hd + 1].to_broadcast([P, NT, HEAD]),
                                ALU.subtract).then_inc(*step("rw_y2", L, ft, hd))
            now("rw_ysq", L, ft)
            chain(v.tensor_reduce(st(1), y1, AX.X, ALU.add))
            v.tensor_scalar(st(1), st(1), 1.0 / HEAD, GN_EPS, ALU.mult, ALU.add).then_inc(*step("rw_var", L, ft))
            now("rw_rstd", L, ft)
            chain(v.tensor_tensor(y0, y0, wide(st(1)), ALU.mult))
            row = lambda i: gn_rows[:, i, ft * P:(ft + 1) * P].unsqueeze(1).to_broadcast([P, NT, P])
            chain(v.tensor_tensor(yt[:, 0, :, :], yt[:, 0, :, :], row(0), ALU.mult))
            chain(v.tensor_tensor(yt[:, 0, :, :], yt[:, 0, :, :], row(1), ALU.add))
            chain(v.tensor_tensor(y1, th(v_tok[:, :, :]), wide(bonus[:, :, :].rearrange("p t d -> p (t d)")), ALU.mult))
            chain(v.tensor_tensor(yt[:, 0, :, :], yt[:, 0, :, :], yt[:, 1, :, :], ALU.add))
            now("rwg_done", L, ft)
            v.tensor_tensor(yt[:, 0, :, :], yt[:, 0, :, :], ps[banks_of.get(("rwg", L, ft), 0)][:, :].rearrange("p (t n) -> p t n", n=P),
                            ALU.mult).then_inc(*step("rw_gated", L, ft))

        @block.tensor
        def _(pe):
            turn = [0]
            holder = {}
            at_slot = [0]
            at_group = [0]

            def take(key, freed_by):
                b = turn[0] % 8
                turn[0] += 1
                if b in holder:
                    pe.wait_ge(*after(*holder[b]))
                holder[b] = freed_by
                banks_of[key] = b
                return ps[b]

            def dense(name, x, feature_major, freed, own_x=None):
                gname, slots, widths = groups[at_group[0]]
                assert gname == name, (gname, name)
                at_group[0] += 1
                n_tiles = len(widths)
                out_b = [take((*name, m), freed(m)) for m in range(n_tiles)]
                for i in range(len(slots)):
                    n = at_slot[0]
                    at_slot[0] += 1
                    last_slot = i == len(slots) - 1
                    r = n % SPLIT_RING
                    pe.wait_ge(*after("w_rest_ready", n))
                    for kk in range(2):
                        k = 2 * i + kk
                        if own_x is not None:
                            own_x(k)
                        for m in range(n_tiles):
                            for xp, wp in ((0, 0), (1, 0), (0, 1)):
                                first = k == 0 and (xp, wp) == (0, 0)
                                last = last_slot and kk == 1 and (xp, wp) == (0, 1)
                                if feature_major:
                                    w = widths[m]
                                    o = out_b[m][0:w, :]
                                    l_ = w_split[wp][:, r, kk, m * P:m * P + w]
                                    r_ = x[xp][:, k, :]
                                else:
                                    o = out_b[m][:, :]
                                    l_ = x[xp][:, k, m * P:(m + 1) * P]
                                    r_ = w_split[wp][:, r, kk, :]
                                ins = nc.tensor.matmul(o, l_, r_, start=first, stop=last)
                                if last:
                                    ins.then_inc(*step("dense_done", *name, m))
                    if last_slot:
                        slot_free[n] = ("dense_done", *name, n_tiles - 1)
                    else:
                        ins.then_inc(*step("w_used", n))
                        slot_free[n] = ("w_used", n)
                    yield

            def run(g):
                for _ in g:
                    pass

            def to_feature_major(L, q):
                for t in range(NT):
                    pe.wait_ge(*after("xn_ready", L, q, t))
                for k in range(KD):
                    b = take(("hT", L, q, k), ("hT_raw", L, q, k))
                    for t in range(NT):
                        ins = nc.tensor.transpose(b[:, t * P:(t + 1) * P], h_tok[:, t, k * P:(k + 1) * P], ident())
                    ins.then_inc(*step("hT_done", L, q, k))

            def ffn(L, f, q):
                for g in range(FT // 2):
                    if g == 0:
                        for k in range(KD):
                            pe.wait_ge(*after("hT_rest", *q, k))
                    run(dense(("up", L, f, g), hT, True,
                              lambda m: ("silu_done", L, f, g, m) if m < 2 else ("act_raw", L, f, g, m - 2)))

                def arrived(k):
                    pe.wait_ge(*after("act_rest", L, f, k))

                for half in range(2):
                    run(dense(("down", L, f, half), aT, False, lambda m: ("res_sum", L, f, half, m),
                              own_x=arrived if half == 0 else None))

            pe.wait_ge(*after("const_in"))
            to_feature_major(0, -1)
            for L in range(DEPTH):
                pe.wait_ge(*after("par_in", L))
                b = take(("par", L), ("par_done", L))
                nc.tensor.transpose(b[:, 0:P], par[:, :], ident()).then_inc(*step("par_T", L))

                ffn(L, 0, (0, -1) if L == 0 else (L - 1, 3))
                to_feature_major(L, 0)
                for k in range(KD):
                    pe.wait_ge(*after("hT_rest", L, 0, k))

                for n in range(3):
                    run(dense(("sb", L, n), hT, n < 2, lambda m: ("sb_in", L, n, m)))
                for m in range(4):
                    for n in range(3):
                        pe.wait_ge(*after("sb_in", L, n, m))
                for h in range(4):
                    zb = {}
                    for kb in range(3, -1, -1):
                        zb[kb] = take(("sbz", L, h, kb), ("sb_exp", L, h, kb))
                        nc.tensor.matmul(zb[kb][:, kb * P:SEQ], sb_k[:, h, kb * P:(kb + 1) * P], sb_q[:, h, kb * P:SEQ],
                                         start=True, stop=False, skip_group_check=True).then_inc(*step("sbz_done", L, h, kb))
                    for kb in range(3, -1, -1):
                        pe.wait_ge(*after("sb_sp", L, h, kb))
                        for k2 in range(kb, 4):
                            ins = nc.tensor.matmul(zb[kb][:, k2 * P:SEQ], cons[:, K_NTRI if k2 == kb else K_NONE, :],
                                                   sb_sp[:, k2, k2 * P:SEQ], start=False, stop=k2 == 3, skip_group_check=True)
                        ins.then_inc(*step("sb_logit", L, h, kb))
                    o = take(("sby", L, h), ("sb_y", L, h))
                    for kb in range(4):
                        pe.wait_ge(*after("sb_att", L, h, kb))
                        ins = nc.tensor.matmul(o[:, kb * P:SEQ], sb_v[:, kb, h * P:(h + 1) * P], sb_att[:, kb, kb * P:SEQ],
                                               start=kb == 0, stop=kb == 3, skip_group_check=True)
                    ins.then_inc(*step("sby_done", L, h))

                for n in range(4):
                    run(dense(("hg", L, n), hT, n < 2, lambda m: ("hg_bf", L, m) if n == 1 else ("hg_in", L, n, m)))
                for m in range(4):
                    pe.wait_ge(*after("hg_kx", L, m))
                    pe.wait_ge(*after("hg_in", L, 0, m))
                for lev in range(-1, len(HG_LEVELS)):
                    if lev >= 0:
                        pe.wait_ge(*after("hg_K", L, lev))
                    for t in range(NT):
                        b = take(("hga", L, lev, t), ("hg_att", L, lev, t))
                        for h in range(4):
                            kk_, qq_ = (hg_k, hg_q) if lev < 0 else (hg_K, hg_Q)
                            ins = nc.tensor.matmul(b[:, h * P:(h + 1) * P], kk_[:, h, t * P:(t + 1) * P],
                                                   qq_[:, h, t * P:(t + 1) * P], start=True, stop=True)
                        ins.then_inc(*step("hga_done", L, lev, t))
                pe.wait_ge(*after("hg_K", L, 99))
                for t in range(NT):
                    b = take(("hgk", L, t), ("hg_ktok", L, t))
                    for h in range(4):
                        ins = nc.tensor.transpose(b[:, h * P:(h + 1) * P], hg_K[:, h, t * P:(t + 1) * P], ident())
                    ins.then_inc(*step("hgk_done", L, t))
                for t in range(NT - 1):
                    pe.wait_ge(*after("hg_ktok", L, t))
                    b = take(("hgd", L, t), ("hg_state", L, t, 3))
                    for h in range(4):
                        ins = nc.tensor.matmul(b[:, h * P:(h + 1) * P], hg_p[:, t, h * P:(h + 1) * P],
                                               hg_v[:, t, h * P:(h + 1) * P], start=True, stop=True)
                    ins.then_inc(*step("hgd_done", L, t))
                for t in range(NT):
                    b = take(("hgo", L, t), ("hg_o", L, t))
                    pe.wait_ge(*after("hg_att", L, len(HG_LEVELS) - 1, t))
                    if t:
                        pe.wait_ge(*after("hg_state", L, t - 1, 3))
                    for h in range(4):
                        ins = nc.tensor.matmul(b[:, h * P:(h + 1) * P], hg_att[:, t, h, :], hg_v[:, t, h * P:(h + 1) * P],
                                               start=True, stop=t == 0)
                        if t:
                            ins = nc.tensor.matmul(b[:, h * P:(h + 1) * P], hg_Q[:, h, t * P:(t + 1) * P],
                                                   hg_S[:, t, h, :], start=False, stop=True)
                    ins.then_inc(*step("hgo_done", L, t))
                run(dense(("lora", L), hT, True, lambda m: ("lora_in", L, m)))
                for t in range(NT):
                    pe.wait_ge(*after("hg_ytok", L, t))
                    b = take(("hgt", L, t), ("hg_y", L, t))
                    for h in range(4):
                        ins = nc.tensor.transpose(b[:, h * P:(h + 1) * P], hg_o_buf(t)[:, h * P:(h + 1) * P], ident())
                    ins.then_inc(*step("hgt_done", L, t))
                run(dense(("rkv", L, 0), hT, True, lambda m: ("rkv_in", L, 0, m)))
                for ft in range(4):
                    rwkv_set_pe(pe, take, L, ft)
                    if ft < 3:
                        run(dense(("rkv", L, ft + 1), hT, True, lambda m: ("rkv_in", L, ft + 1, m)))
                for half in range(2):
                    for br in range(3):
                        run(dense(("gate", L, half, br), hT, True, lambda m: ("gate_sig", L, half, br, m)))
                        for k in range(4):
                            pe.wait_ge(*after("yT_rest", L, half, br, k))
                        run(dense(("branch", L, half, br), yT, True, lambda m: ("merge", L, half, br, m)))

                def merged(k):
                    pe.wait_ge(*after("mT_rest", L, k))

                for half in range(2):
                    run(dense(("out", L, half), mT, False, lambda m: ("res_sum", L, "mix", half, m),
                              own_x=merged if half == 0 else None))
                to_feature_major(L, 1)
                ffn(L, 1, (L, 1))
                to_feature_major(L, 2)
                pe.wait_ge(*after("p_in", L))
                for k in range(2):
                    b = take(("pT", L, k), ("pT_raw", L, k))
                    for t in range(NT):
                        ins = nc.tensor.transpose(b[:, t * P:(t + 1) * P], p_tok[:, t, k * P:(k + 1) * P], ident())
                    ins.then_inc(*step("pT_done", L, k))
                for k in range(KD):
                    pe.wait_ge(*after("hT_rest", L, 2, k))
                for k in range(2):
                    pe.wait_ge(*after("pT_rest", L, k))
                for half in range(2):
                    run(dense(("pgate", L, half), hT, False, lambda m: ("ple_sig", L, half, m)))
                    run(dense(("pproj", L, half), pT, False, lambda m: ("ple_mul", L, half, m)))
                if L < DEPTH - 1:
                    to_feature_major(L, 3)

        @block.gpsimd
        def _(pool):
            nc.gpsimd.memset(zero[:, :], 0.0).then_inc(*step("zero_set"))
            pool.wait_ge(*after("zero_set"))
            for n, (pieces, g, i) in enumerate(slot_list):
                r, q = n % RAW_RING, n % SPLIT_RING
                w = sum(x[2] for x in pieces)
                pool.wait_ge(*after(f"w_in{r}", n))
                if n >= SPLIT_RING:
                    pool.wait_ge(*after(*slot_free[n - SPLIT_RING]))
                nc.gpsimd.tensor_tensor(w_split[0][:, q, :, 0:w], w_raw[:, r, :, 0:w],
                                        zero[:, 0:1].unsqueeze(2).to_broadcast([P, 2, w]), ALU.add).then_inc(*step("w_high", n))
                pool.wait_ge(*after("w_high", n))
                nc.gpsimd.tensor_tensor(w_split[1][:, q, :, 0:w], w_raw[:, r, :, 0:w],
                                        w_split[0][:, q, :, 0:w].bitcast(F32), ALU.subtract).then_inc(*step("w_rest_ready", n))

        @block.sync
        def _(sp):
            x_t = a["x"][0].rearrange("(t p) d -> p t d", p=P)
            sp.dma_start(h_tok[:, :, :], x_t).then_inc(*step("x_in", by=16))
            sp.dma_start(cons[:, :, :].rearrange("p a n -> p (a n)"), a["consts"]).then_inc(*step("const_in", by=16))

            def load_weights(upto):
                while done[0] < min(upto, len(slot_list)):
                    n = done[0]
                    done[0] += 1
                    pieces, g, i = slot_list[n]
                    r = n % RAW_RING
                    if n >= RAW_RING:
                        sp.wait_ge(*after("w_rest_ready", n - RAW_RING))
                    for src, at, w in pieces:
                        sp.dma_start(w_raw[:, r, :, at:at + w], src).then_inc(*step(f"w_in{r}", n, by=16))

            done = [0]
            load_weights(len(slot_list))

        @block.scalar
        def _(act):
            def chain(ins):
                ins.then_inc(*step("act_chain"))
                act.wait_ge(*after("act_chain"))

            def now(name, *index):
                act.wait_ge(*after(name, *index))

            def load_params(L):
                if L:
                    now("par_T", L - 1)
                rows = [(R_LNG, a["ln_g"][L].rearrange("q (k p) -> (q k) p", p=P), 32),
                        (R_LNB, a["ln_b"][L].rearrange("q (k p) -> (q k) p", p=P), 32),
                        (R_MU, a["rw_mu"][L, 0:14 * P].rearrange("(k p) -> k p", p=P), 14)]
                for row, key in ((R_W0, "rw_w0"), (R_A0, "rw_a0"), (R_KK, "rw_k_k"), (R_KA, "rw_k_a")):
                    rows.append((row, a[key][L].rearrange("(k p) -> k p", p=P), 4))
                rows.append((R_RK, a["rw_r_k"][L].rearrange("(k h) n -> k (h n)", h=2), 4))
                rows.append((R_LB, a["hg_lb_raw"].rearrange("l (k p) -> (l k) p", p=P), 8))
                for row, src, n in rows:
                    act.dma_start(par[row:row + n, :], src).then_inc(*step("par_in", L, by=16))
                act.dma_start(par[R_MU + 14:R_MU + 15, 0:32], a["rw_mu"][L:L + 1, 14 * P:14 * P + 32]).then_inc(*step("par_in", L, by=16))

            def param_columns(L):
                now("par_T", L)
                if L:
                    now("hT_raw", L - 1, 3, KD - 1)
                nc.scalar.activation(parT[:, :], ps[banks_of.get(("par", L), 0)][:, 0:P], ACT.Copy).then_inc(*step("par_done", L))
                now("par_done", L)

            def feature_major(L, q, scale):
                for k in range(KD):
                    b = ps[banks_of.get(("hT", L, q, k), 0)]
                    now("hT_done", L, q, k)
                    if k >= 2:
                        now("hT_rest", L, q, k - 2)
                    if scale:
                        g = parT[:, R_LNG + 8 * q + k:R_LNG + 8 * q + k + 1]
                        o = parT[:, R_LNB + 8 * q + k:R_LNB + 8 * q + k + 1]
                        nc.scalar.activation(h_raw[:, k % 2, :], b[:, :], ACT.Identity, bias=o, scale=g).then_inc(
                            *step("hT_raw", L, q, k))
                    else:
                        nc.scalar.activation(h_raw[:, k % 2, :], b[:, :], ACT.Copy).then_inc(*step("hT_raw", L, q, k))

            def norm(L, q, last=False):
                f = {0: 0, 1: "mix", 2: 1, 3: "ple"}[q]
                last_of = {0: ("dense_done", "down", L, 0, 1, 3), 1: ("dense_done", "out", L, 1, 3),
                           2: ("dense_done", "down", L, 1, 1, 3), 3: ("h_scaled", L, 2, NT - 1)}[q]
                now(*last_of)
                act.dma_start(ln_rows[:, 0, :], a["ln_g"][L, q:q + 1, :].partition_broadcast(P)).then_inc(*step("rows_in", L, q, by=16))
                act.dma_start(ln_rows[:, 1, :], a["ln_b"][L, q:q + 1, :].partition_broadcast(P)).then_inc(*step("rows_in", L, q, by=16))
                if q == 2:
                    act.dma_start(p_tok[:, :, :], a["p"][L, 0].rearrange("(t p) d -> p t d", p=P)).then_inc(*step("p_in", L, by=16))
                for t in range(NT):
                    now("ln_var", L, q, t)
                nc.scalar.activation(ln_rstd[:, :, :], ln_mv[:, :, 1:2], ACT.Sqrt).then_inc(*step("ln_sqrt", L, q))
                if not last:
                    feature_major(L, q, True)

            def ffn(L, f):
                for g in range(FT // 2):
                    for m in range(2):
                        now("dense_done", "up", L, f, g, m)
                        if g:
                            now("act_raw", L, f, g - 1, m)
                        b = ps[banks_of.get(("up", L, f, g, m), 0)]
                        nc.scalar.activation(silu[:, m, :], b[:, :], ACT.Silu).then_inc(*step("silu_done", L, f, g, m))

            now("par_zero")
            load_params(0)
            now("x_in")
            feature_major(0, -1, False)
            for L in range(DEPTH):
                if L:
                    load_params(L)
                param_columns(L)
                ffn(L, 0)
                norm(L, 0)

                for t in range(NT):
                    now("h_scaled", L, 0, t)
                    act.dma_start(h_dram[t, :, :], h_tok[:, t, :]).then_inc(*step("h_out", L, by=16))
                now("h_out", L)
                for n in range(3):
                    dst = (sb_q, sb_k, sb_v)[n]
                    for m in range(4):
                        now("dense_done", "sb", L, n, m)
                        b = ps[banks_of.get(("sb", L, n, m), 0)]
                        nc.scalar.activation(dst[:, m, :], b[:, :], ACT.Copy, scale=P ** -0.5 if n == 0 else 1.0).then_inc(
                            *step("sb_in", L, n, m))
                for h in range(4):
                    for kb in range(3, -1, -1):
                        b = ps[banks_of.get(("sbz", L, h, kb), 0)]
                        cols = slice(kb * P, SEQ)
                        now("sbz_done", L, h, kb)
                        if kb < 2:
                            now("sb_sp0", L, h, kb + 2)
                        elif h:
                            now("sb_sp0", L, h - 1, kb - 2)
                        chain(nc.scalar.activation(sb_e[:, kb % 2, cols], b[:, cols], ACT.Abs))
                        chain(nc.scalar.activation(sb_e[:, kb % 2, cols], sb_e[:, kb % 2, cols], ACT.Exp, scale=-1.0))
                        nc.scalar.activation(sb_e[:, kb % 2, cols], sb_e[:, kb % 2, cols], ACT.Ln, bias=1.0).then_inc(
                            *step("sb_ln", L, h, kb))
                    for kb in range(3, -1, -1):
                        b = ps[banks_of.get(("sbz", L, h, kb), 0)]
                        cols = slice(kb * P, SEQ)
                        now("sb_logit", L, h, kb)
                        if h:
                            now("sby_done", L, h - 1)
                        nc.scalar.activation(sb_att[:, kb, cols], b[:, cols], ACT.Exp).then_inc(*step("sb_exp", L, h, kb))
                    now("sby_done", L, h)
                    nc.scalar.activation(y_raw[:, 0, h, :], ps[banks_of.get(("sby", L, h), 0)][:, :], ACT.Copy).then_inc(
                        *step("sb_y", L, h))

                act.dma_start(hg_row[:, :], a["hg_norm_g"][L:L + 1, :].partition_broadcast(P)).then_inc(*step("hg_row_in", L, by=16))
                if L:
                    now("lb_abs", L)
                    chain(nc.scalar.activation(lbT[:, 12:16], lbT[:, 12:16], ACT.Exp, scale=-1.0))
                    nc.scalar.activation(lbT[:, 12:16], lbT[:, 12:16], ACT.Ln, bias=1.0).then_inc(*step("lb_ln", L))
                for m in range(4):
                    now("dense_done", "hg", L, 0, m)
                    nc.scalar.activation(hg_q[:, m, :], ps[banks_of.get(("hg", L, 0, m), 0)][:, :], ACT.Sigmoid).then_inc(
                        *step("hg_in", L, 0, m))
                for m in range(4):
                    e = hg_e[:, m % 2, 0:SEQ]
                    e2 = hg_e[:, m % 2, SEQ:2 * SEQ]
                    b = ps[banks_of.get(("hg", L, 1, m), 0)]
                    now("dense_done", "hg", L, 1, m)
                    if m >= 2:
                        now("hg_lf", L, m - 2)
                    chain(nc.scalar.activation(e, b[:, :], ACT.Abs))
                    chain(nc.scalar.activation(e, e, ACT.Exp, scale=-1.0))
                    nc.scalar.activation(e, e, ACT.Ln, bias=1.0).then_inc(*step("hg_ln1", L, m))
                    now("hg_b", L, m)
                    chain(nc.scalar.activation(e2, hg_x[:, m, :], ACT.Abs))
                    chain(nc.scalar.activation(e2, e2, ACT.Exp, scale=-1.0))
                    nc.scalar.activation(e2, e2, ACT.Ln, bias=1.0).then_inc(*step("hg_ln2", L, m))
                    now("hg_bf", L, m)
                    nc.scalar.activation(hg_k[:, m, :], hg_Q[:, m, :], ACT.Exp).then_inc(*step("hg_kx", L, m))
                for m in range(4):
                    now("dense_done", "hg", L, 2, m)
                    nc.scalar.activation(hg_v[:, m, :], ps[banks_of.get(("hg", L, 2, m), 0)][:, :], ACT.Copy).then_inc(
                        *step("hg_in", L, 2, m))
                for m in range(4):
                    now("dense_done", "hg", L, 3, m)
                    nc.scalar.activation(hg_g[:, m, :], ps[banks_of.get(("hg", L, 3, m), 0)][:, :], ACT.Silu).then_inc(
                        *step("hg_in", L, 3, m))
                for lev in range(len(HG_LEVELS)):
                    hgt, n = HG_LEVELS[lev], 2048 // (2 * HG_LEVELS[lev])
                    if lev == 0:
                        for m in range(4):
                            now("hg_lf", L, m)
                    else:
                        now("hg_pupd", L, lev - 1)
                        now("hg_K", L, lev - 1)
                    view = lambda t_: t_[:, :, :].rearrange("p h (n two s) -> p (h n) two s", two=2, s=hgt)
                    nc.scalar.activation(hg_e[:, 0, :].rearrange("p (n s) -> p n s", s=hgt), view(hg_p)[:, :, 1, :], ACT.Exp).then_inc(
                        *step("hg_ep", L, lev))
                    if lev:
                        nc.scalar.activation(hg_e[:, 1, :].rearrange("p (n s) -> p n s", s=hgt), view(hg_x)[:, :, 0, :], ACT.Exp).then_inc(
                            *step("hg_ex", L, lev))
                now("hg_pupd", L, len(HG_LEVELS) - 1)
                nc.scalar.activation(hg_p[:, :, :], hg_p[:, :, :], ACT.Exp).then_inc(*step("hg_expP", L))
                nc.scalar.activation(hg_x[:, :, :], hg_x[:, :, :], ACT.Exp).then_inc(*step("hg_expX", L))
                now("hg_glast", L)
                for t in range(NT):
                    now("hgk_done", L, t)
                    nc.scalar.activation(hg_p[:, t, :], ps[banks_of.get(("hgk", L, t), 0)][:, :], ACT.Copy).then_inc(
                        *step("hg_ktok", L, t))
                for t in range(NT):
                    now("hgo_done", L, t)
                    if t >= 2:
                        now("hg_ms", L, t - 2)
                    nc.scalar.activation(hg_e[:, t % 2, 0:512], ps[banks_of.get(("hgo", L, t), 0)][:, :], ACT.Square).then_inc(
                        *step("hg_osq", L, t))
                for t in range(NT):
                    now("hg_ms", L, t)
                nc.scalar.activation(gn_small("hg_r"), gn_small("hg_r"), ACT.Sqrt, scale=1.0 / P).then_inc(*step("hg_sqrt", L))
                for t in range(NT):
                    now("hgt_done", L, t)
                    nc.scalar.activation(y_raw[:, 1, :, t * P:(t + 1) * P],
                                         ps[banks_of.get(("hgt", L, t), 0)][:, :].rearrange("p (h n) -> p h n", h=4),
                                         ACT.Copy).then_inc(*step("hg_y", L, t))

                act.dma_start(w_up[0:64, :], a["rw_w_up"][L]).then_inc(*step("rw_wts", L, by=16))
                act.dma_start(w_up[64:128, :], a["rw_a_up"][L]).then_inc(*step("rw_wts", L, by=16))
                act.dma_start(g_up[:, 0, :], a["rw_g_up"][L, 0:128, :]).then_inc(*step("rw_wts", L, by=16))
                act.dma_start(g_up[0:32, 1, :], a["rw_g_up"][L, 128:160, :]).then_inc(*step("rw_wts", L, by=16))
                act.dma_start(gn_rows[:, 0, :], a["rw_gn_g"][L:L + 1, :].partition_broadcast(P)).then_inc(*step("rw_wts", L, by=16))
                act.dma_start(gn_rows[:, 1, :], a["rw_gn_b"][L:L + 1, :].partition_broadcast(P)).then_inc(*step("rw_wts", L, by=16))
                for m in range(3):
                    w = (P, P, 32)[m]
                    now("dense_done", "lora", L, m)
                    if m == 0:
                        now("rw_u0", L)
                    nc.scalar.activation(rw_u[0:w, m, 1:SEQ + 1], ps[banks_of.get(("lora", L, m), 0)][0:w, :], ACT.Copy).then_inc(
                        *step("lora_in", L, m))
                now("lora_mix", L, 0)
                nc.scalar.activation(lora_x[0:64, 0, :], lora_x[0:64, 0, :], ACT.Tanh).then_inc(*step("lora_tanh", L))
                now("lora_mix", L, 2)
                nc.scalar.activation(lora_x[:, 1, :], lora_x[:, 1, :], ACT.Sigmoid).then_inc(*step("lora_act0", L))
                nc.scalar.activation(lora_x[0:32, 2, :], lora_x[0:32, 2, :], ACT.Sigmoid).then_inc(*step("lora_act", L))
                for ft in range(4):
                    for m in range(3):
                        now("dense_done", "rkv", L, ft, m)
                        if ft:
                            now("rkv_mix", L, ft - 1, m)
                        else:
                            now("lora_mix", L, m)
                        nc.scalar.activation(rw_u[:, m, 1:SEQ + 1], ps[banks_of.get(("rkv", L, ft, m), 0)][:, :], ACT.Copy).then_inc(
                            *step("rkv_in", L, ft, m))
                    now("rww_done", L, ft)
                    if ft:
                        now("rw_csm", L, ft - 1)
                        now("rw_b_", L, ft - 1)
                    nc.scalar.activation(rw_sw[:, :], ps[banks_of.get(("rww", L, ft), 0)][:, :], ACT.Sigmoid,
                                         bias=parT[:, R_W0 + ft:R_W0 + ft + 1]).then_inc(*step("rw_sw", L, ft))
                    now("rwa_done", L, ft)
                    nc.scalar.activation(rw_a[:, :], ps[banks_of.get(("rwa", L, ft), 0)][:, :], ACT.Sigmoid,
                                         bias=parT[:, R_A0 + ft:R_A0 + ft + 1]).then_inc(*step("rw_a", L, ft))
                    now("rw_kkr", L, ft)
                    nc.scalar.activation(rw_ss[:, :], rw_kk[:, :], ACT.Square).then_inc(*step("rw_sq", L, ft))
                    now("rw_csm", L, ft)
                    nc.scalar.activation(rw_e1[:, :], rw_cs[:, :], ACT.Exp, scale=-DECAY).then_inc(*step("rw_e1", L, ft))
                    now("rw_e1", L, ft)
                    nc.scalar.activation(rw_cs[:, :], rw_cs[:, :], ACT.Exp, scale=DECAY).then_inc(*step("rw_e2", L, ft))
                    nc.scalar.activation(rw_e3[:, :], rw_e3[:, :], ACT.Exp, scale=-DECAY).then_inc(*step("rw_e3", L, ft))
                    now("rw_ssmax", L, ft)
                    chain(nc.scalar.activation(rw_ss[:, :], rw_ss[:, :], ACT.Ln, scale=SS_SCALE))
                    nc.scalar.activation(rw_ss[:, :], rw_ss[:, :], ACT.Exp, scale=-0.5).then_inc(*step("rw_rn", L, ft))
                    for i in range(4):
                        now("rwt_done", L, ft, i)
                        b = ps[banks_of.get(("rwt", L, ft, i), 0)]
                        if i == 1:
                            dst = rhs[:, :, :, 0:HEAD].rearrange("p d t n -> p t d n")
                        else:
                            dst = {0: v_tok, 2: b_tok, 3: k_tok}[i][:, :, :].rearrange("p t (d n) -> p t d n", d=2)
                        src = b[:, :].rearrange("p (t d n) -> p t d n", t=NT, d=2)
                        if i == 1:
                            for hd in range(2):
                                ins = nc.scalar.activation(rhs[:, hd, :, 0:HEAD], src[:, :, hd, :], ACT.Copy)
                            ins.then_inc(*step("rw_tok", L, ft, i))
                        else:
                            dst = {0: v_tok, 2: b_tok, 3: k_tok}[i]
                            nc.scalar.activation(dst[:, :, :].rearrange("p t n -> p (t n)"), b[:, :], ACT.Copy).then_inc(
                                *step("rw_tok", L, ft, i))
                    now("rwl_done", L, ft)
                    nc.scalar.activation(rhs[:, :, :, HEAD:P].rearrange("p d t n -> p (d t) n"),
                                         ps[banks_of.get(("rwl", L, ft), 0)][:, :].rearrange("p (u n) -> p u n", n=HEAD),
                                         ACT.Copy).then_inc(*step("rw_lakv", L, ft))
                    for hd in range(2):
                        now("rwu_done", L, ft, hd)
                        nc.scalar.activation(xx[:, hd, :, :].rearrange("p t n -> p (t n)"),
                                             ps[banks_of.get(("rwu", L, ft, hd), 0)][:, :], ACT.Copy).then_inc(*step("rw_wu", L, ft, hd))
                    for name, dst in (("p", p_mat), ("d", d_mat)):
                        for cp in range(2):
                            now(f"rw{name}_done", L, ft, cp)
                            nc.scalar.activation(dst.rearrange("p (t two) n -> p t two n", two=2)[:, :, cp, :],
                                                 ps[banks_of.get((f"rw{name}", L, ft, cp), 0)][:, 0:256].rearrange("p (t n) -> p t n", n=HEAD),
                                                 ACT.Copy).then_inc(*step(f"rw_{name}", L, ft, cp))
                    now("rw_y2", L, ft, 1)
                    nc.scalar.activation(yt[:, 1, :, :], yt[:, 0, :, :], ACT.Square).then_inc(*step("rw_ysq", L, ft))
                    now("rw_var", L, ft)
                    chain(nc.scalar.activation(gn_st[:, 1, :, :], gn_st[:, 1, :, :], ACT.Ln))
                    nc.scalar.activation(gn_st[:, 1, :, :], gn_st[:, 1, :, :], ACT.Exp, scale=-0.5).then_inc(*step("rw_rstd", L, ft))
                    now("rwo_done", L, ft)
                    nc.scalar.activation(y_raw[:, 2, ft, :], ps[banks_of.get(("rwo", L, ft), 0)][:, :], ACT.Copy).then_inc(
                        *step("rw_yT", L, ft))

                now("rw_yT", L, 3)
                for half in range(2):
                    for br in range(3):
                        for m in range(4):
                            now("dense_done", "gate", L, half, br, m)
                            if half or br:
                                now("merge", L, *divmod(3 * half + br - 1, 3), m)
                            nc.scalar.activation(gate_s[:, m, :], ps[banks_of.get(("gate", L, half, br, m), 0)][:, :],
                                                 ACT.Sigmoid).then_inc(*step("gate_sig", L, half, br, m))
                now("dense_done", "out", L, 1, 3)
                for t in range(NT):
                    act.dma_start(h_tok[:, t, :], h_dram[t, :, :]).then_inc(*step("h_back", L, by=16))
                norm(L, 1)
                ffn(L, 1)
                norm(L, 2)
                for k in range(2):
                    now("pT_done", L, k)
                    nc.scalar.activation(p_raw[:, k, :], ps[banks_of.get(("pT", L, k), 0)][:, :], ACT.Copy).then_inc(*step("pT_raw", L, k))
                for half in range(2):
                    for m in range(4):
                        now("dense_done", "pgate", L, half, m)
                        if half:
                            now("ple_mul", L, 0, m)
                        nc.scalar.activation(ple_sig[:, m, :], ps[banks_of.get(("pgate", L, half, m), 0)][:, :], ACT.Sigmoid).then_inc(
                            *step("ple_sig", L, half, m))
                norm(L, 3, last=L == DEPTH - 1)
            for t in range(NT):
                now("h_final", t)
                act.dma_start(out[0, t * P:(t + 1) * P, :], h_new[:, t % 2, :]).then_inc(*step(f"stored{t % 2}", t, by=16))
            now("stored0", NT - 2)
            now("stored1", NT - 1)

        @block.vector
        def _(dve):
            def chain(ins):
                ins.then_inc(*step("dve_chain"))
                dve.wait_ge(*after("dve_chain"))

            def now(name, *index):
                dve.wait_ge(*after(name, *index))

            v = nc.vector

            def split(L, q):
                for k in range(KD):
                    now("hT_raw", L, q, k)
                    chain(v.tensor_copy(hT[0][:, k, :], h_raw[:, k % 2, :]))
                    v.tensor_tensor(hT[1][:, k, :], h_raw[:, k % 2, :], hT[0][:, k, :].bitcast(F32), ALU.subtract).then_inc(
                        *step("hT_rest", L, q, k))

            def norm(L, q, last=False):
                for t in range(NT):
                    for half in range(2):
                        v.bn_stats(ln_small[:, t, 6 * half:6 * half + 6], h_tok[:, t, 512 * half:512 * half + 512]).then_inc(
                            *step("bn_done", L, q, t, half))
                    now("bn_done", L, q, t, 1)
                    chain(v.bn_aggr(ln_mv[:, t, :], ln_small[:, t, 0:12]))
                    v.tensor_scalar(ln_mv[:, t, 1:2], ln_mv[:, t, 1:2], LN_EPS, None, ALU.add).then_inc(*step("ln_var", L, q, t))
                now("ln_sqrt", L, q)
                chain(v.reciprocal(ln_rstd[:, :, :], ln_rstd[:, :, :]))
                for t in range(NT):
                    v.tensor_scalar(h_tok[:, t, :], h_tok[:, t, :], ln_mv[:, t, 0:1], ln_rstd[:, t, :], ALU.subtract, ALU.mult).then_inc(
                        *step("xn_ready", L, q, t))
                if last:
                    now("rows_in", L, q)
                    for t in range(NT):
                        now("xn_ready", L, q, t)
                        if t >= 2:
                            now(f"stored{t % 2}", t - 2)
                        chain(v.tensor_tensor(h_new[:, t % 2, :], h_tok[:, t, :], ln_rows[:, 0, :], ALU.mult))
                        v.tensor_tensor(h_new[:, t % 2, :], h_new[:, t % 2, :], ln_rows[:, 1, :], ALU.add).then_inc(*step("h_final", t))
                    return
                split(L, q)
                now("rows_in", L, q)
                chain(v.tensor_scalar(ln_rows[:, :, :], ln_rows[:, :, :], ALPHA, None, ALU.mult))
                now("hT_done", L, q, KD - 1)
                for t in range(NT):
                    chain(v.tensor_tensor(h_tok[:, t, :], h_tok[:, t, :], ln_rows[:, 0, :], ALU.mult))
                    v.tensor_tensor(h_tok[:, t, :], h_tok[:, t, :], ln_rows[:, 1, :], ALU.add).then_inc(*step("h_scaled", L, q, t))

            def ffn(L, f):
                for g in range(FT // 2):
                    for m in range(2):
                        now("silu_done", L, f, g, m)
                        now("dense_done", "up", L, f, g, m + 2)
                        b = ps[banks_of.get(("up", L, f, g, m + 2), 0)]
                        v.tensor_tensor(act_raw[:, m, :], silu[:, m, :], b[:, :], ALU.mult).then_inc(*step("act_raw", L, f, g, m))
                        now("act_raw", L, f, g, m)
                        k = 2 * g + m
                        chain(v.tensor_copy(aT[0][:, k, :], act_raw[:, m, :]))
                        v.tensor_tensor(aT[1][:, k, :], act_raw[:, m, :], aT[0][:, k, :].bitcast(F32), ALU.subtract).then_inc(
                            *step("act_rest", L, f, k))
                residual("down", L, f, (f,))

            def residual(name, L, f, extra):
                for half in range(2):
                    for m in range(4):
                        now("dense_done", name, L, *extra, half, m)
                        b = ps[banks_of.get((name, L, *extra, half, m), 0)]
                        z = h_tok[:, m, 512 * half:512 * half + 512]
                        v.scalar_tensor_tensor(z, b[:, :], 0.5 if name == "down" else 1.0, z, ALU.mult, ALU.add).then_inc(
                            *step("res_sum", L, f, half, m))
                now("res_sum", L, f, 1, 3)

            v.memset(par[:, :], 0.0).then_inc(*step("par_zero"))
            now("x_in")
            for t in range(NT):
                v.tensor_scalar(ln_mv[:, t, 0:1], h_tok[:, t, 0:1], 1.0, None, ALU.mult).then_inc(*step("xn_ready", 0, -1, t))
            split(0, -1)
            now("hT_done", 0, -1, KD - 1)
            chain(v.tensor_scalar(h_tok[:, :, :], h_tok[:, :, :], ALPHA, None, ALU.mult))
            for L in range(DEPTH):
                ffn(L, 0)
                norm(L, 0)
                for h in range(4):
                    for kb in range(3, -1, -1):
                        b = ps[banks_of.get(("sbz", L, h, kb), 0)]
                        cols = slice(kb * P, SEQ)
                        diag = slice(kb * P, kb * P + P)
                        now("sb_ln", L, h, kb)
                        if h:
                            now("sb_logit", L, h - 1, 0)
                        v.scalar_tensor_tensor(sb_sp[:, kb, cols], b[:, cols], 0.0, sb_e[:, kb % 2, cols], ALU.max, ALU.add).then_inc(
                            *step("sb_sp0", L, h, kb))
                        now("sb_sp0", L, h, kb)
                        v.tensor_tensor(sb_sp[:, kb, diag], sb_sp[:, kb, diag], cons[:, K_CAUSAL, :], ALU.mult).then_inc(
                            *step("sb_sp", L, h, kb))
                    for kb in range(3, -1, -1):
                        diag = slice(kb * P, kb * P + P)
                        now("sb_exp", L, h, kb)
                        v.scalar_tensor_tensor(sb_att[:, kb, diag], sb_att[:, kb, diag], 3e38, cons[:, K_CAUSAL, :], ALU.min,
                                               ALU.mult).then_inc(*step("sb_att", L, h, kb))
                now("sb_y", L, 3)
                now("par_done", L)
                lb_log, lb_rest, lb_s = lbT[:, 0:4], lbT[:, 4:8], lbT[:, 8:12]
                if L == 0:
                    v.memset(lb_log, LOG_ZERO)
                    v.memset(lb_rest, 0.0).then_inc(*step("lb_set", L))
                else:
                    chain(v.tensor_tensor(lb_s, parT[:, R_LB + 4:R_LB + 8], parT[:, R_LB:R_LB + 4], ALU.subtract))
                    v.scalar_tensor_tensor(lbT[:, 12:16], lb_s, -1.0, lb_s, ALU.mult, ALU.max).then_inc(*step("lb_abs", L))
                    now("lb_ln", L)
                    chain(v.scalar_tensor_tensor(lb_rest, lb_s, 0.0, lbT[:, 12:16], ALU.max, ALU.add))
                    chain(v.tensor_tensor(lb_log, lb_s, lb_rest, ALU.subtract))
                    v.tensor_scalar(lb_rest, lb_rest, -1.0, None, ALU.mult).then_inc(*step("lb_set", L))
                now("lb_set", L)
                for m in range(4):
                    b = ps[banks_of.get(("hg", L, 1, m), 0)]
                    e, e2 = hg_e[:, m % 2, 0:SEQ], hg_e[:, m % 2, SEQ:2 * SEQ]
                    col = lbT[:, m:m + 1]
                    rest = lbT[:, 4 + m:5 + m]
                    now("hg_ln1", L, m)
                    chain(v.scalar_tensor_tensor(hg_p[:, m, :], b[:, :], 0.0, e, ALU.min, ALU.subtract))
                    chain(v.tensor_scalar(hg_p[:, m, :], hg_p[:, m, :], rest, None, ALU.add))
                    v.tensor_scalar(hg_x[:, m, :], hg_p[:, m, :], col, None, ALU.subtract).then_inc(*step("hg_b", L, m))
                    v.tensor_tensor(hg_Q[:, m, :], hg_p[:, m, :], b[:, :], ALU.subtract).then_inc(*step("hg_bf", L, m))
                    now("hg_ln2", L, m)
                    v.scalar_tensor_tensor(hg_p[:, m, :], hg_p[:, m, :], col, e2, ALU.max, ALU.add).then_inc(*step("hg_lf", L, m))
                now("hg_lf", L, 3)
                for m in range(4):
                    now("hg_kx", L, m)
                chain(v.memset(hg_x[:, :, :], 0.0))
                chain(v.memset(hg_att[:, :, :, :], 0.0))
                chain(v.tensor_copy(hg_Q[:, :, :], hg_q[:, :, :]))
                chain(v.tensor_copy(hg_K[:, :, :], hg_k[:, :, :]))

                def keep_pairs(lev):
                    for t in range(NT):
                        now("hga_done", L, lev, t)
                        if lev >= 0:
                            now("hg_att", L, lev - 1, t)
                        mask = ident() if lev < 0 else cons[:, K_HG + lev, :]
                        b = ps[banks_of.get(("hga", L, lev, t), 0)]
                        v.copy_predicated(hg_att[:, t, :, :], mask.bitcast(I32).unsqueeze(1).to_broadcast([P, 4, P]),
                                          b[:, :].rearrange("p (h n) -> p h n", h=4)).then_inc(*step("hg_att", L, lev, t))

                for lev in range(len(HG_LEVELS)):
                    hgt = HG_LEVELS[lev]
                    n = 2048 // (2 * hgt)
                    view = lambda t_: t_[:, :, :].rearrange("p h (n two s) -> p (h n) two s", two=2, s=hgt)
                    e0 = hg_e[:, 0, :].rearrange("p (n s) -> p n s", s=hgt)
                    e1 = hg_e[:, 1, :].rearrange("p (n s) -> p n s", s=hgt)
                    now("hg_ep", L, lev)
                    if lev:
                        now("hg_ex", L, lev)
                        now("hga_done", L, lev - 1, NT - 1)
                    v.tensor_tensor(view(hg_Q)[:, :, 1, :], view(hg_q)[:, :, 1, :], e0, ALU.mult).then_inc(*step("hg_Qh", L, lev))
                    if lev:
                        now("hg_Qh", L, lev)
                        v.tensor_tensor(view(hg_K)[:, :, 0, :], view(hg_k)[:, :, 0, :], e1, ALU.mult).then_inc(*step("hg_K", L, lev))
                    else:
                        v.tensor_copy(view(hg_K)[:, :, 0, :], view(hg_k)[:, :, 0, :]).then_inc(*step("hg_K", L, lev))
                    chain(v.tensor_tensor(view(hg_x)[:, :, 0, :], view(hg_x)[:, :, 0, :],
                                          view(hg_p)[:, :, 1, hgt - 1:hgt].to_broadcast([P, n, hgt]), ALU.add))
                    v.tensor_tensor(view(hg_p)[:, :, 1, :], view(hg_p)[:, :, 1, :],
                                    view(hg_p)[:, :, 0, hgt - 1:hgt].to_broadcast([P, n, hgt]), ALU.add).then_inc(*step("hg_pupd", L, lev))
                    now("hg_pupd", L, lev)
                    keep_pairs(lev - 1)
                keep_pairs(len(HG_LEVELS) - 1)
                now("hg_expX", L)
                now("hg_expP", L)
                now("hga_done", L, len(HG_LEVELS) - 1, NT - 1)
                v.tensor_tensor(hg_Q[:, :, :], hg_q[:, :, :], hg_p[:, :, :], ALU.mult)
                v.tensor_copy(lbT[:, 8:24].rearrange("p (h t) -> p h t", h=4),
                              hg_p[:, :, :].rearrange("p h (t n) -> p h t n", n=P)[:, :, :, P - 1]).then_inc(*step("hg_glast", L))
                v.tensor_tensor(hg_K[:, :, :], hg_k[:, :, :], hg_x[:, :, :], ALU.mult).then_inc(*step("hg_K", L, 99))
                now("hg_K", L, 99)
                for t in range(NT - 1):
                    now("hgd_done", L, t)
                    b = ps[banks_of.get(("hgd", L, t), 0)]
                    for h in range(4):
                        if t == 0:
                            v.tensor_copy(hg_S[:, 1, h, :], b[:, h * P:(h + 1) * P]).then_inc(*step("hg_state", L, t, h))
                        else:
                            v.scalar_tensor_tensor(hg_S[:, t + 1, h, :], hg_S[:, t, h, :], lbT[:, 8 + 4 * h + t:9 + 4 * h + t],
                                                   b[:, h * P:(h + 1) * P], ALU.mult, ALU.add).then_inc(*step("hg_state", L, t, h))
                    now("hg_state", L, t, 3)
                hr = gn_small("hg_r")
                for t in range(NT):
                    now("hg_osq", L, t)
                    v.tensor_reduce(hr[:, t, :], hg_e[:, t % 2, 0:512].rearrange("p (h n) -> p h n", h=4), AX.X, ALU.add).then_inc(
                        *step("hg_ms0", L, t))
                    now("hg_ms0", L, t)
                    v.tensor_scalar(hr[:, t, :], hr[:, t, :], HG_EPS * P, None, ALU.add).then_inc(*step("hg_ms", L, t))
                now("hg_sqrt", L)
                chain(v.reciprocal(hr, hr))
                now("hg_row_in", L)
                for t in range(NT):
                    o = hg_o_buf(t)
                    b = ps[banks_of.get(("hgo", L, t), 0)]
                    v.tensor_tensor(o.rearrange("p (h n) -> p h n", h=4), b[:, :].rearrange("p (h n) -> p h n", h=4),
                                    hr[:, t, :].unsqueeze(2).to_broadcast([P, 4, P]), ALU.mult).then_inc(*step("hg_o", L, t))
                    now("hg_o", L, t)
                    chain(v.tensor_tensor(o, o, hg_row[:, :], ALU.mult))
                    now("hg_in", L, 3, t)
                    v.tensor_tensor(o, o, hg_g[:, t, :], ALU.mult).then_inc(*step("hg_ytok", L, t))

                now("hg_y", L, 3)
                chain(v.memset(rw_u[:, :, 0:1], 0.0))
                chain(v.memset(rk_sel[:, :, :], 0.0))
                for hd in range(2):
                    v.tensor_copy(rk_sel[unit(hd), :, hd], parT[unit(hd), R_RK:R_RK + 4])
                v.memset(rw_keep[:, 0:1], 0.0).then_inc(*step("rw_u0", L))
                for m in range(3):
                    w = (P, P, 32)[m]
                    now("lora_in", L, m)
                    if m:
                        now("lora_mix", L, m - 1)
                    shift_mix(v, chain, rw_u[0:w, m, :], rw_d[0:w, :], lora_x[0:w, m, :], parT[0:w, R_MU + 12 + m:R_MU + 13 + m]).then_inc(
                        *step("lora_mix", L, m))
                for ft in range(4):
                    rwkv_set_dve(v, now, chain, L, ft)

                now("rw_yT", L, 3)
                for half in range(2):
                    for br in range(3):
                        if half or br:
                            now("dense_done", "branch", L, *divmod(3 * half + br - 1, 3), 3)
                        for k in range(4):
                            chain(v.tensor_copy(yT[0][:, k, :], y_raw[:, br, k, :]))
                            v.tensor_tensor(yT[1][:, k, :], y_raw[:, br, k, :], yT[0][:, k, :].bitcast(F32), ALU.subtract).then_inc(
                                *step("yT_rest", L, half, br, k))
                        for m in range(4):
                            now("gate_sig", L, half, br, m)
                            now("dense_done", "branch", L, half, br, m)
                            b = ps[banks_of.get(("branch", L, half, br, m), 0)]
                            dst = m_acc[:, 4 * half + m, :]
                            v.tensor_tensor(dst if br == 0 else m_tmp[:, :], gate_s[:, m, :], b[:, :], ALU.mult).then_inc(
                                *step("merge", L, half, br, m))
                            now("merge", L, half, br, m)
                            if br:
                                chain(v.tensor_tensor(dst, dst, m_tmp[:, :], ALU.add))
                            if br == 2:
                                k = 4 * half + m
                                chain(v.tensor_copy(mT[0][:, k, :], dst))
                                v.tensor_tensor(mT[1][:, k, :], dst, mT[0][:, k, :].bitcast(F32), ALU.subtract).then_inc(
                                    *step("mT_rest", L, k))
                now("h_back", L)
                residual("out", L, "mix", ())
                norm(L, 1)
                ffn(L, 1)
                norm(L, 2)
                for k in range(2):
                    now("pT_raw", L, k)
                    chain(v.tensor_copy(pT[0][:, k, :], p_raw[:, k, :]))
                    v.tensor_tensor(pT[1][:, k, :], p_raw[:, k, :], pT[0][:, k, :].bitcast(F32), ALU.subtract).then_inc(
                        *step("pT_rest", L, k))
                for half in range(2):
                    for m in range(4):
                        now("ple_sig", L, half, m)
                        now("dense_done", "pproj", L, half, m)
                        b = ps[banks_of.get(("pproj", L, half, m), 0)]
                        z = h_tok[:, m, 512 * half:512 * half + 512]
                        v.tensor_tensor(ple_pr[:, :], ple_sig[:, m, :], b[:, :], ALU.mult).then_inc(*step("ple_mul", L, half, m))
                        now("ple_mul", L, half, m)
                        chain(v.tensor_tensor(z, z, ple_pr[:, :], ALU.add))
                norm(L, 3, last=L == DEPTH - 1)



INPUTS = ["x", "p", "ln_g", "ln_b", "ffn1_wg", "ffn1_wu", "ffn1_wd", "w_in", "rw_mu", "rw_w0", "rw_w_up", "rw_a0",
          "rw_a_up", "rw_g_up", "rw_k_k", "rw_k_a", "rw_r_k", "rw_gn_g", "rw_gn_b", "hg_lb_raw", "hg_norm_g",
          "w_br_rw", "w_br_sb", "w_br_hg", "w_out", "ffn2_wg", "ffn2_wu", "ffn2_wd", "ple_gate", "ple_proj"]


def program(make, arrays):
    counts, banks_of = {}, {}
    for _ in range(2):
        nc = make()
        a = {n: nc.dram_tensor(f"in_{n}", v.shape, F32, kind="ExternalInput").ap() for n, v in arrays.items()}
        out = nc.dram_tensor("out_0_dram", (1, SEQ, D), F32, kind="ExternalOutput").ap()
        build(nc, a, out, counts, banks_of)
    return nc


def kernel(**inputs):
    import concourse.bacc as _bacc
    from concourse.bass_utils import run_bass_kernel_spmd as _run

    arrays = {n: np.ascontiguousarray(inputs[n]) for n in INPUTS}
    arrays["consts"] = constants()
    nc = program(lambda: _bacc.Bacc("TRN2", target_bir_lowering=False, num_devices=1), arrays)
    r = _run(nc, [{f"in_{n}": v for n, v in arrays.items()}], core_ids=[0])
    return r.results[0]["out_0_dram"]
```

```python
from contextlib import ExitStack

import numpy as np

import concourse.bass as bass
from concourse import mybir

F32 = mybir.dt.float32
F32R = mybir.dt.float32r
I32 = mybir.dt.int32
ALU = mybir.AluOpType
ACT = mybir.ActivationFunctionType
AX = mybir.AxisListType

P = 128
D = 1024
SEQ = 512
DEPTH = 2
PLE = 256
FF = 2816
KD = D // P
NT = SEQ // P
FT = FF // P
ALPHA = (2 * DEPTH) ** 0.25
LN_EPS = 1e-5
GN_EPS = 64e-5
HG_EPS = 1e-5
HALF = P // 2
HEAD = 64
NC = SEQ // HEAD
DECAY = float(np.exp(-0.5))
LOG_ZERO = -1e30
SS_SCALE = float(2.0 ** 20)

C_R, C_K, C_V, C_W, C_XG = 0, 512, 1024, 1536, 1664
C_SB = 1824
C_HG = C_SB + 1536
C_GATE = C_HG + 2048

K_ID, K_NTRI, K_NONE, K_ONES64, K_CAUSAL, K_RW, K_RX, K_HG = 0, 1, 2, 3, 4, 5, 7, 13
RX_LEVELS = [1, 2, 4, 8, 16, 32]
HG_LEVELS = [1, 2, 4, 8, 16, 32, 64]
N_CONST = K_HG + len(HG_LEVELS)

R_LNG, R_LNB, R_MU, R_W0, R_A0, R_KK, R_KA, R_RK, R_LB = 0, 32, 64, 79, 83, 87, 91, 95, 99

FILL_MANY = {"pairs": [0], "level": [1, 3], "after": [0, 1], "chunk": [1, 3, 5]}
FILL_FEW = {"pairs": [0], "level": [5], "after": [1], "chunk": []}
FILL_PLACES = [FILL_MANY, FILL_MANY, FILL_FEW, FILL_FEW]

RAW_RING = 3
SPLIT_RING = 3


def constants():
    i = np.arange(P)[:, None]
    j = np.arange(P)[None, :]
    blocks = [i == j, -1.0 * (i >= j), -np.ones((P, P)), i // 64 == j // 64, i < j,
              (i // 64 == j // 64) & (i < j), (i // 64 == j // 64) & (i <= j)]
    pair = lambda late, early, h: (late // (2 * h) == early // (2 * h)) & (late // h % 2 == 1) & (early // h % 2 == 0)
    blocks += [pair(i, j, h) for h in RX_LEVELS]
    blocks += [pair(j, i, h) for h in HG_LEVELS]
    return np.concatenate([np.asarray(b, np.float32) for b in blocks], axis=1)


def dense_groups(a):
    groups = []

    def add(name, pieces, rows, widths):
        slots = []
        for s in range(rows // 256):
            slots.append([(w[s * 256:(s + 1) * 256, c:c + n].rearrange("(k p) n -> p k n", p=P), at, n)
                          for w, c, at, n in pieces])
        groups.append((name, slots, widths))

    four = [P] * 4
    for L in range(DEPTH):
        for f in range(2):
            wg, wu, wd = ((a["ffn1_wg"], a["ffn1_wu"], a["ffn1_wd"]), (a["ffn2_wg"], a["ffn2_wu"], a["ffn2_wd"]))[f]
            if f == 1:
                w_in = a["w_in"][L]

                def cols(name, c):
                    add(name, [(w_in, c, 0, 512)], D, four)

                for n in range(3):
                    cols(("sb", L, n), C_SB + 512 * n)
                for n in range(4):
                    cols(("hg", L, n), C_HG + 512 * n)
                add(("lora", L), [(w_in, C_W, 0, 288)], D, [P, P, 32])
                for ft in range(4):
                    add(("rkv", L, ft), [(w_in, c + P * ft, P * n, P) for n, c in enumerate((C_R, C_K, C_V))],
                        D, [P] * 3)
                for half in range(2):
                    for br, (key, col) in enumerate((("w_br_sb", 1), ("w_br_hg", 2), ("w_br_rw", 0))):
                        cols(("gate", L, half, br), C_GATE + D * col + 512 * half)
                        add(("branch", L, half, br), [(a[key][L], 512 * half, 0, 512)], 512, four)
                for half in range(2):
                    add(("out", L, half), [(a["w_out"][L], 512 * half, 0, 512)], D, four)
            for g in range(FT // 2):
                add(("up", L, f, g), [(wg[L], 256 * g, 0, 256), (wu[L], 256 * g, 256, 256)], D, four)
            for half in range(2):
                add(("down", L, f, half), [(wd[L], 512 * half, 0, 512)], FF, four)
        for half in range(2):
            add(("pgate", L, half), [(a["ple_gate"][L], 512 * half, 0, 512)], D, four)
            add(("pproj", L, half), [(a["ple_proj"][L], 512 * half, 0, 512)], PLE, four)
    return groups


def build(nc, a, out, counts, banks_of):
    ctx = ExitStack()
    with ctx:
        sems, reached = {}, {}

        def sem_of(name):
            if name not in sems:
                sems[name] = ctx.enter_context(nc.semaphore(name))
                reached[name] = 0
            return sems[name]

        def step(name, *index, by=1):
            s = sem_of(name)
            reached[name] += by
            counts[(name, *index)] = reached[name]
            return s, by

        def after(name, *index):
            return sem_of(name), counts.get((name, *index), 1)

        def sb(stack, name, shape, dt=F32):
            return stack.enter_context(nc.sbuf_tensor(name, shape, dt))

        cons = sb(ctx, "cons", [P, N_CONST, P])
        hT = [sb(ctx, "hT_hi", [P, KD, SEQ], F32R), sb(ctx, "hT_lo", [P, KD, SEQ], F32R)]
        w_raw = sb(ctx, "w_raw", [P, RAW_RING, 2, 512])
        w_split = [sb(ctx, "w_hi", [P, SPLIT_RING, 2, 512], F32R), sb(ctx, "w_lo", [P, SPLIT_RING, 2, 512], F32R)]
        zero = sb(ctx, "zero", [P, 1])
        ln_eps = sb(ctx, "ln_eps", [P, 1])
        par = sb(ctx, "par", [P, P])
        parT = sb(ctx, "parT", [P, P])
        lbT = sb(ctx, "lbT", [P, 24])
        ln_small = sb(ctx, "ln_small", [P, NT, 16])
        ln_mv = sb(ctx, "ln_mv", [P, NT, 2])
        ln_rstd = sb(ctx, "ln_rstd", [P, NT, 1])

        ps = [ctx.enter_context(nc.psum_tensor(f"ps{b}", [P, 512], F32)) for b in range(8)]

        def ident():
            return cons[:, K_ID, :]

        with ExitStack() as own:
            h_tok = sb(own, "h_tok", [P, NT, D])
            with ExitStack() as o2:
                aT = [sb(o2, "aT_hi", [P, FT, SEQ], F32R), sb(o2, "aT_lo", [P, FT, SEQ], F32R)]
                silu = sb(o2, "silu", [P, 2, SEQ])
                act_raw = sb(o2, "act_raw", [P, 2, SEQ])
                p_tok = sb(o2, "p_tok", [P, NT, PLE])
                pT = [sb(o2, "pT_hi", [P, 2, SEQ], F32R), sb(o2, "pT_lo", [P, 2, SEQ], F32R)]
            with ExitStack() as o2:
                ln_rows = sb(o2, "ln_rows", [P, 2, D])
                h_raw = sb(o2, "h_raw", [P, KD, SEQ])
                h_new = sb(o2, "h_new", [P, 2, D])
                ple_sig = sb(o2, "ple_sig", [P, 4, 512])
                ple_pr = sb(o2, "ple_pr", [P, 512])
        with ExitStack() as own:
            y_raw = sb(own, "y_raw", [P, 3, 4, SEQ])
            sb_sp, sb_att = y_raw[:, 1, :, :], y_raw[:, 2, :, :]
            o3 = ExitStack()
            rw_u = sb(o3, "rw_u", [P, 3, SEQ + 1])
            rw_d = sb(o3, "rw_d", [P, SEQ])
            lora_x = sb(o3, "lora_x", [P, 3, SEQ])
            with ExitStack() as o1:
                hg_q = sb(o1, "hg_q", [P, 4, SEQ])
                hg_k = sb(o1, "hg_k", [P, 4, SEQ])
                hg_p = sb(o1, "hg_p", [P, 4, SEQ])
                hg_x = sb(o1, "hg_x", [P, 4, SEQ])
                hg_v = sb(o1, "hg_v", [P, NT, 512])
                hg_g = sb(o1, "hg_g", [P, NT, 512])
                hg_e = sb(o1, "hg_e", [P, 2, 1024])
                with ExitStack() as o2:
                    sb_q = sb(o2, "sb_q", [P, 4, SEQ])
                    sb_k = sb(o2, "sb_k", [P, 4, SEQ])
                    sb_v = sb(o2, "sb_v", [P, NT, 512])
                    sb_e = sb(o2, "sb_e", [P, 4, SEQ])
                with ExitStack() as o2:
                    hg_Q = sb(o2, "hg_Q", [P, 4, SEQ])
                    hg_K = sb(o2, "hg_K", [P, 4, SEQ])
                    hg_att = sb(o2, "hg_att", [P, NT, 4, P])
                    hg_S = sb(o2, "hg_S", [P, NT, 4, P])
                    hg_row = sb(o2, "hg_row", [P, 512])
            with ExitStack() as o2:
                rkv = sb(o2, "rkv", [P, 3, SEQ])
                w_up = sb(o2, "w_up", [P, 512])
                g_up = sb(o2, "g_up", [P, 2, 512])
                gn_rows = sb(o2, "gn_rows", [P, 2, 512])
                rw_sw = sb(o2, "rw_sw", [P, SEQ])
                rw_a = sb(o2, "rw_a", [P, SEQ])
                rw_cs = sb(o2, "rw_cs", [P, SEQ])
                rw_e3 = sb(o2, "rw_e3", [P, SEQ])
                bm = sb(o2, "bm", [P, 2, NT, 2, P])
                rw_e1 = sb(o2, "rw_e1", [P, SEQ])
                rw_kk = sb(o2, "rw_kk", [P, SEQ])
                rw_ss = sb(o2, "rw_ss", [P, SEQ])
                rw_keep = sb(o2, "rw_keep", [P, SEQ])
                km = sb(o2, "km", [P, 2, NT, 2, P])
                inv = sb(o2, "inv", [P, 2, NT, P])
                invT = sb(o2, "invT", [P, 2, NT, P])
                rw_dec = sb(o2, "rw_dec", [P, 2, SEQ])
                ar = sb(o2, "ar", [P, NT, 2, P])
                b_inv = sb(o2, "b_inv", [P, SEQ])
                k_inv = sb(o2, "k_inv", [P, SEQ])
                b_tok = sb(o2, "b_tok", [P, NT, P])
                k_tok = sb(o2, "k_tok", [P, NT, P])
                yt = sb(o2, "yt", [P, 2, NT, P])
                rhs = sb(o2, "rhs", [P, 2, NT, P])
                xx = sb(o2, "xx", [P, 2, NT, P])
                v_tok = sb(o2, "v_tok", [P, NT, P])
                r_dec = sb(o2, "r_dec", [P, NT, P])
                s_pre = sb(o2, "s_pre", [P, HEAD])
                e_last = sb(o2, "e_last", [P, NC])
                bonus = sb(o2, "bonus", [P, NT, 2])
                rk_sel = sb(o2, "rk_sel", [P, 4, 2])
                gn_st = sb(o2, "gn_st", [P, 2, NT, 2])
            rw_bd, rw_kd = rw_dec[:, 0, :], rw_dec[:, 1, :]
            rw_b, rw_k2 = rw_ss, rw_sw
            q_eff = inv[:, 0, :, :].rearrange("p t n -> p (t n)")
            p_mat = inv[:, 1, :, :].rearrange("p t (c n) -> p (t c) n", c=2)
            d_mat = rhs[:, 0, :, :].rearrange("p t (c n) -> p (t c) n", c=2)
            s_all = rhs[:, 1, :, :].rearrange("p t (c n) -> p (t c) n", c=2)
            o3.close()
            with ExitStack() as o2:
                yT = [sb(o2, "yT_hi", [P, 4, SEQ], F32R), sb(o2, "yT_lo", [P, 4, SEQ], F32R)]
                gate_s = sb(o2, "gate_s", [P, 4, SEQ])
                m_tmp = sb(o2, "m_tmp", [P, SEQ])
                m_acc = sb(o2, "m_acc", [P, KD, SEQ])
                mT = [sb(o2, "mT_hi", [P, KD, SEQ], F32R), sb(o2, "mT_lo", [P, KD, SEQ], F32R)]
        h_dram = nc.dram_tensor("h_dram", (NT, P, D), F32).ap()

        groups = dense_groups(a)
        slot_list = [(pieces, g, i) for g in groups for i, pieces in enumerate(g[1])]
        slot_free = {}

        block = ctx.enter_context(nc.Block())

        def hg_decay(lev, which):
            buf = y_raw[:, 2, :, :].rearrange("p a n -> p (a n)") if lev % 2 else hg_e[:, :, :].rearrange("p a n -> p (a n)")
            return buf[:, 1024 * which:1024 * which + 1024]

        def hg_o_buf(t):
            return hg_x[:, t, :]

        def unit(hd):
            return slice(HEAD * hd, HEAD * hd + HEAD)

        def columns(x, lev, which):
            return x.rearrange("p (n two s) -> p n two s", two=2, s=RX_LEVELS[lev])[:, :, which, :]

        def of_tiles(x, height, which):
            return x.rearrange("p t (n two s) -> p t n two s", two=2, s=height)[:, :, :, which, :]

        def bank_halves(b, height, which):
            return of_tiles(b[:, :].rearrange("p (t n) -> p t n", n=P), height, which)

        def core_banks_of(ft):
            return range(3, 8) if ft < 2 else range(4, 8)

        def rates_pe(pe, take, L, ft):
            if ft == 0:
                pe.wait_ge(*after("lora_act", L))
                pe.wait_ge(*after("rw_wts", L))
            for name, rows, m in (("rww", slice(0, 64), "rw_sw"), ("rwa", slice(64, 128), "rw_a")):
                b = take((name, L, ft), (m, L, ft), core_banks_of(ft - 1))
                nc.tensor.matmul(b[:, :], w_up[rows, ft * P:(ft + 1) * P], lora_x[rows, 0, :], start=True,
                                 stop=True).then_inc(*step(f"{name}_done", L, ft))

        def key_norms_pe(pe, take, L, ft):
            pe.wait_ge(*after("rw_sq", L, ft))
            b = take(("rwss", L, ft), ("rw_ssmax", L, ft), core_banks_of(ft - 1))
            nc.tensor.matmul(b[:, :], cons[:, K_ONES64, :], rw_ss[:, :], start=True,
                             stop=True).then_inc(*step("rwss_done", L, ft))

        def output_gate_pe(pe, take, L, ft):
            b = take(("rwg", L, ft), ("rw_gated", L, ft), core_banks_of(ft + 1))
            for t in range(NT):
                nc.tensor.matmul(b[:, t * P:(t + 1) * P], lora_x[:, 1, t * P:(t + 1) * P], g_up[:, 0, ft * P:(ft + 1) * P],
                                 start=True, stop=False)
                ins = nc.tensor.matmul(b[:, t * P:(t + 1) * P], lora_x[0:32, 2, t * P:(t + 1) * P],
                                       g_up[0:32, 1, ft * P:(ft + 1) * P], start=False, stop=True)
            ins.then_inc(*step("rwg_done", L, ft))

        def output_pe(pe, take, L, ft):
            pe.wait_ge(*after("rw_gated", L, ft))
            b = take(("rwo", L, ft), ("rw_yT", L, ft), core_banks_of(ft + 1))
            for t in range(NT):
                ins = nc.tensor.transpose(b[:, t * P:(t + 1) * P], yt[:, 0, t, :], ident())
            ins.then_inc(*step("rwo_done", L, ft))

        def rwkv_core_pe(pe, take_bank, used_last, advance, L, ft):
            def between(place, index):
                if index in FILL_PLACES[ft][place]:
                    advance(1)

            def take(key, freed_by):
                return take_bank(key, freed_by, core_banks_of(ft))

            pe.wait_ge(*after("rkv_mix", L, ft, 2))
            pe.wait_ge(*after("rw_kd", L, ft))
            def token_major(i, src):
                b = take(("rwt", L, ft, i), ("rw_tok", L, ft, i))
                for t in range(NT):
                    ins = nc.tensor.transpose(b[:, t * P:(t + 1) * P], src(t), ident())
                ins.then_inc(*step("rwt_done", L, ft, i))

            token_major(2, lambda t: rw_bd[:, t * P:(t + 1) * P])
            token_major(3, lambda t: rw_kd[:, t * P:(t + 1) * P])
            token_major(1, lambda t: ar[:, t, 0, :])
            between("pairs", 0)
            for i, src in enumerate((b_inv, k_inv)):
                for hd in range(2):
                    for tp in range(2):
                        b = take(("rwm", L, ft, i, hd, tp), ("rw_mask", L, ft, i, hd, tp))
                        for t in (2 * tp, 2 * tp + 1):
                            ins = nc.tensor.matmul(b[:, (t % 2) * 256:(t % 2) * 256 + 256], src[unit(hd), t * P:(t + 1) * P],
                                                   ar[unit(hd), t, :, :].rearrange("p a n -> p (a n)"), start=True, stop=True)
                        ins.then_inc(*step("rwm_done", L, ft, i, hd, tp))
                between("pairs", 1 + i)
            if ft:
                output_gate_pe(pe, take_bank, L, ft - 1)
            token_major(0, lambda t: rkv[:, 2, t * P:(t + 1) * P])
            b = take(("rwb", L, ft), ("rw_bonus", L, ft))
            pe.wait_ge(*after("rk_sel", L))
            pe.wait_ge(*after("rw_rk", L, ft))
            for t in range(NT):
                ins = nc.tensor.matmul(b[:, 2 * t:2 * t + 2], rw_keep[:, t * P:(t + 1) * P], rk_sel[:, ft, :], start=True, stop=True)
            ins.then_inc(*step("rwb_done", L, ft))
            for lev in range(len(RX_LEVELS)):
                for hd in range(2):
                    b = take(("rwx", L, ft, lev, hd), ("rw_x", L, ft, lev, hd))
                    if lev == 0:
                        for tp in range(2):
                            pe.wait_ge(*after("rw_mask", L, ft, 0, hd, tp))
                    else:
                        pe.wait_ge(*after("rw_inv", L, ft, lev - 1, hd))
                        pe.wait_ge(*after("rw_invT", L, ft, lev - 1, hd))
                    for t in range(NT):
                        ins = nc.tensor.matmul(b[:, t * P:(t + 1) * P], bm[:, hd, t, 0, :],
                                               ident() if lev == 0 else inv[:, hd, t, :], start=True, stop=True)
                    ins.then_inc(*step("rwx_done", L, ft, lev, hd))
                if lev == 0:
                    if ft:
                        output_pe(pe, take_bank, L, ft - 1)
                    if ft < 3:
                        rates_pe(pe, take_bank, L, ft + 1)
                    continue
                between("level", lev)
                for hd in range(2):
                    pe.wait_ge(*after("rw_x", L, ft, lev, hd))
                    if lev < len(RX_LEVELS) - 1:
                        b = take(("rwi", L, ft, lev, hd), ("rw_inv", L, ft, lev, hd))
                        for t in range(NT):
                            ins = nc.tensor.matmul(b[:, t * P:(t + 1) * P], invT[:, hd, t, :], xx[:, hd, t, :], start=True, stop=True)
                        ins.then_inc(*step("rwi_done", L, ft, lev, hd))
                    b = take(("rwj", L, ft, lev, hd), ("rw_invT", L, ft, lev, hd))
                    for t in range(NT):
                        ins = nc.tensor.matmul(b[:, t * P:(t + 1) * P], xx[:, hd, t, :], invT[:, hd, t, :], start=True, stop=True)
                    ins.then_inc(*step("rwj_done", L, ft, lev, hd))
                if lev == 4 and ft < 3:
                    key_norms_pe(pe, take_bank, L, ft + 1)
            between("after", 0)
            for hd in range(2):
                for tp in range(2):
                    pe.wait_ge(*after("rw_mask", L, ft, 1, hd, tp))
            pe.wait_ge(*after("rw_tok", L, ft, 0))
            b = take(("rwl", L, ft), ("rw_lakv", L, ft))
            for hd in range(2):
                for t in range(NT):
                    c = (hd * NT + t) * HEAD
                    ins = nc.tensor.matmul(b[:, c:c + HEAD], km[:, hd, t, 0, :], v_tok[:, t, unit(hd)], start=True, stop=True)
            ins.then_inc(*step("rwl_done", L, ft))
            pe.wait_ge(*after("rw_lakv", L, ft))
            pe.wait_ge(*after("rw_tok", L, ft, 1))
            for hd in range(2):
                b = take(("rwu", L, ft, hd), ("rw_wu", L, ft, hd))
                pe.wait_ge(*after("rw_invT", L, ft, len(RX_LEVELS) - 1, hd))
                for t in range(NT):
                    ins = nc.tensor.matmul(b[:, t * P:(t + 1) * P], invT[:, hd, t, :], rhs[:, hd, t, :], start=True, stop=True)
                ins.then_inc(*step("rwu_done", L, ft, hd))
            for hd in range(2):
                pe.wait_ge(*after("rw_wu", L, ft, hd))
            pe.wait_ge(*after("rw_tok", L, ft, 3))
            between("after", 1)
            for cp in range(2):
                b = take(("rwp", L, ft, cp), ("rw_p", L, ft, cp))
                cs = slice(HEAD * cp, HEAD * cp + HEAD)
                for hd in range(2):
                    for t in range(NT):
                        ins = nc.tensor.matmul(b[unit(hd), t * HEAD:(t + 1) * HEAD], xx[cs, hd, t, 0:HEAD], b_tok[cs, t, unit(hd)],
                                               start=True, stop=True)
                ins.then_inc(*step("rwp_done", L, ft, cp))
            for cp in range(2):
                b = take(("rwd", L, ft, cp), ("rw_d", L, ft, cp))
                cs = slice(HEAD * cp, HEAD * cp + HEAD)
                for hd in range(2):
                    for t in range(NT):
                        nc.tensor.matmul(b[unit(hd), t * HEAD:(t + 1) * HEAD], b_tok[cs, t, unit(hd)], xx[cs, hd, t, HEAD:P],
                                         start=True, stop=False)
                        ins = nc.tensor.matmul(b[unit(hd), t * HEAD:(t + 1) * HEAD], k_tok[cs, t, unit(hd)], v_tok[cs, t, unit(hd)],
                                               start=False, stop=True)
                ins.then_inc(*step("rwd_done", L, ft, cp))
            b = take(("rwq", L, ft), ("rw_q", L, ft))
            for hd in range(2):
                for t in range(NT):
                    ins = nc.tensor.matmul(b[unit(hd), t * P:(t + 1) * P], xx[:, hd, t, 0:HEAD], bm[:, hd, t, 1, :],
                                           start=True, stop=True)
            ins.then_inc(*step("rwq_done", L, ft))
            y_bank = [take(("rwy", L, ft, hd), ("rw_y2", L, ft, hd)) for hd in range(2)]
            rest = [x for x in core_banks_of(ft) if x not in [banks_of[("rwy", L, ft, hd)] for hd in range(2)]]
            pe.wait_ge(*after("rw_p", L, ft, 1))
            for c in range(1, NC):
                pe.wait_ge(*after("rw_state", L, ft, c - 1))
                if c < NC - 1:
                    b = take_bank(("rws", L, ft, c), ("rw_state", L, ft, c), rest)
                    for hd in range(2):
                        ins = nc.tensor.matmul(b[unit(hd), 0:HEAD], p_mat[unit(hd), c, :], s_all[unit(hd), c, :], start=True, stop=True)
                    ins.then_inc(*step("rws_done", L, ft, c))
                if c == 1:
                    pe.wait_ge(*after("rw_q", L, ft))
                t = c // 2
                if c % 2 == 0 or c == 1:
                    for hd in range(2):
                        y = y_bank[hd][:, t * HEAD:(t + 1) * HEAD]
                        nc.tensor.matmul(y, bm[:, hd, t, 1, :], xx[:, hd, t, HEAD:P], start=t == 0, stop=False, skip_group_check=True)
                        nc.tensor.matmul(y, km[:, hd, t, 1, :], v_tok[:, t, unit(hd)], start=False, stop=False, skip_group_check=True)
                half = slice(HEAD * (c % 2), HEAD * (c % 2) + HEAD)
                for hd in range(2):
                    ins = nc.tensor.matmul(y_bank[hd][half, t * HEAD:(t + 1) * HEAD], q_eff[unit(hd), c * HEAD:(c + 1) * HEAD],
                                           s_all[unit(hd), c, :], start=False, stop=c == NC - 1, skip_group_check=True)
                    if c == NC - 1:
                        ins.then_inc(*step("rwy_done", L, ft, hd))
                between("chunk", c)
            for hd in range(2):
                used_last(("rwy", L, ft, hd))

        def gn_small(which):
            return ln_small[:, :, 0:4]

        def shift_mix(v, chain, u, d, dst, mu):
            chain(v.tensor_tensor(d, u[:, 0:SEQ], u[:, 1:SEQ + 1], ALU.subtract))
            return v.scalar_tensor_tensor(dst, d, mu, u[:, 1:SEQ + 1], ALU.mult, ALU.add)

        def prepare_dve(v, now, chain, L, ft):
            if ft:
                now("rwt_done", L, ft - 1, 0)
            for m in range(3):
                now("rkv_in", L, ft, m)
                if m:
                    now("rkv_mix", L, ft, m - 1)
                u = rw_u[:, m, :]
                mu = parT[:, R_MU + 4 * m + ft:R_MU + 4 * m + ft + 1]
                v.tensor_tensor(rw_d[:, :], u[:, 0:SEQ], u[:, 1:SEQ + 1], ALU.subtract).then_inc(*step("rkv_dif", L, ft, m))
                yield
                now("rkv_dif", L, ft, m)
                v.scalar_tensor_tensor(rkv[:, m, :], rw_d[:, :], mu, u[:, 1:SEQ + 1], ALU.mult, ALU.add).then_inc(
                    *step("rkv_mix", L, ft, m))
                yield
            now("rkv_mix", L, ft, 2)
            v.tensor_scalar(rw_kk[:, :], rkv[:, 1, :], parT[:, R_KK + ft:R_KK + ft + 1], None, ALU.mult).then_inc(*step("rw_kkr", L, ft))
            yield
            chain(v.memset(rw_e1[:, :], 1.0))
            chain(v.memset(rw_e1[:, :].rearrange("p (c n) -> p c n", n=HEAD)[:, :, 0:1], 0.0))
            yield
            now("rw_sw", L, ft)
            v.tensor_tensor_scan(rw_cs[:, :], rw_e1[:, :], rw_sw[:, :], 0.0, ALU.mult, ALU.add).then_inc(*step("rw_cs", L, ft))
            yield
            now("rw_cs", L, ft)
            v.tensor_tensor(rw_e3[:, :], rw_cs[:, :], rw_sw[:, :], ALU.subtract).then_inc(*step("rw_csm", L, ft))
            yield
            now("rw_a", L, ft)
            now("rw_csm", L, ft)
            if ft:
                now("rwb_done", L, ft - 1)
            v.tensor_scalar(rw_k2[:, :], rw_a[:, :], 1.0, parT[:, R_KA + ft:R_KA + ft + 1], ALU.subtract, ALU.mult).then_inc(
                *step("rw_ka", L, ft))
            yield
            now("rw_ka", L, ft)
            v.scalar_tensor_tensor(rw_k2[:, :], rw_k2[:, :], 1.0, rkv[:, 1, :], ALU.add, ALU.mult).then_inc(*step("rw_k2", L, ft))
            yield
            now("rw_k2", L, ft)
            v.tensor_tensor(rw_keep[:, :], rkv[:, 0, :], rw_k2[:, :], ALU.mult).then_inc(*step("rw_rk", L, ft))
            yield
            now("rwss_done", L, ft)
            v.tensor_scalar(rw_ss[:, :], ps[banks_of.get(("rwss", L, ft), 0)][:, :], 1e-24, None, ALU.max).then_inc(*step("rw_ssmax", L, ft))
            yield
            tiles = lambda x: x[:, :].rearrange("p (t n) -> p t n", n=P)
            now("rw_e3", L, ft)
            if ft:
                now("rwt_done", L, ft - 1, 1)
                now("rwm_done", L, ft - 1, 1, 1, 1)
            v.tensor_tensor(ar[:, :, 1, :], rkv[:, 0, :].rearrange("p (t n) -> p t n", n=P), tiles(rw_e1), ALU.mult)
            yield
            v.tensor_tensor(k_inv[:, :], rw_k2[:, :], rw_cs[:, :], ALU.mult).then_inc(*step("rw_ki", L, ft))
            yield
            now("rw_ki", L, ft)
            chunk = lambda x: x[:, :].rearrange("p (c n) -> p c n", n=HEAD)
            last = chunk(rw_e1)[:, :, HEAD - 1:HEAD].to_broadcast([P, NC, HEAD])
            v.tensor_tensor(chunk(rw_kd), chunk(k_inv), last, ALU.mult)
            yield
            now("rw_rn", L, ft)
            v.scalar_tensor_tensor(rw_kk[:, :], rw_kk[:, :], SS_SCALE ** 0.5, rw_ss[:, :], ALU.mult, ALU.mult).then_inc(
                *step("rw_kkn", L, ft))
            yield
            now("rw_kkn", L, ft)
            v.tensor_tensor(rw_b[:, :], rw_kk[:, :], rw_a[:, :], ALU.mult).then_inc(*step("rw_b_", L, ft))
            yield
            v.scalar_tensor_tensor(ar[:, :, 0, :], tiles(rw_kk), -1.0, tiles(rw_e3), ALU.mult, ALU.mult)
            yield
            now("rw_b_", L, ft)
            v.tensor_tensor(b_inv[:, :], rw_b[:, :], rw_cs[:, :], ALU.mult).then_inc(*step("rw_bi", L, ft))
            yield
            now("rw_bi", L, ft)
            v.tensor_tensor(chunk(rw_bd), chunk(b_inv), last, ALU.mult).then_inc(*step("rw_kd", L, ft))
            yield

        def core_dve(v, now, chain, L, ft):
            if ft:
                now("rw_q", L, ft - 1)
                now("rw_state", L, ft - 1, NC - 2)
            now("rw_kd", L, ft)
            v.tensor_copy(r_dec[:, :, :], ar[:, :, 1, :])
            v.tensor_copy(e_last[:, :], rw_e1[:, :].rearrange("p (c n) -> p c n", n=HEAD)[:, :, HEAD - 1]).then_inc(*step("rw_kept", L, ft))
            for i, dst in enumerate((bm, km)):
                for hd in range(2):
                    for tp in range(2):
                        now("rwm_done", L, ft, i, hd, tp)
                        b = ps[banks_of.get(("rwm", L, ft, i, hd, tp), 0)]
                        mask = cons[:, K_RW:K_RW + 2, :].rearrange("p a n -> p (a n)")
                        v.tensor_tensor(dst[:, hd, 2 * tp:2 * tp + 2, :, :].rearrange("p t a n -> p t (a n)"),
                                        b[:, :].rearrange("p (t n) -> p t n", t=2), mask.unsqueeze(1).to_broadcast([P, 2, 256]),
                                        ALU.mult).then_inc(*step("rw_mask", L, ft, i, hd, tp))
                if ft:
                    (variance_dve, gated_dve)[i](v, now, chain, L, ft - 1)
            now("rwb_done", L, ft)
            v.tensor_copy(bonus[:, :, :], ps[banks_of.get(("rwb", L, ft), 0)][:, 0:8].rearrange("p (t d) -> p t d", d=2)).then_inc(
                *step("rw_bonus", L, ft))
            four = lambda m_: m_.unsqueeze(1).to_broadcast([P, NT, P])
            following = prepare_dve(v, now, chain, L, ft + 1) if ft < 3 else iter(())
            for lev in range(len(RX_LEVELS)):
                for hd in range(2):
                    now("rwx_done", L, ft, lev, hd)
                    b = ps[banks_of.get(("rwx", L, ft, lev, hd), 0)]
                    if lev == 0:
                        v.tensor_tensor(xx[:, hd, :, :], b[:, :].rearrange("p (t n) -> p t n", t=NT), four(cons[:, K_RX + lev, :]),
                                        ALU.mult).then_inc(*step("rw_x", L, ft, lev, hd))
                    else:
                        hgt = RX_LEVELS[lev]
                        v.memset(of_tiles(xx[:, hd, :, :], hgt, 1)[:, :, :, 0:hgt // 2], 0.0)
                        mask = columns(cons[:, K_RX + lev, :], lev, 0).unsqueeze(1).to_broadcast([P, NT, HALF // hgt, hgt])
                        v.tensor_tensor(of_tiles(xx[:, hd, :, :], hgt, 0), bank_halves(b, hgt, 0), mask,
                                        ALU.mult).then_inc(*step("rw_x", L, ft, lev, hd))
                    if lev:
                        next(following, None)
                    if lev == 0:
                        now("rw_x", L, ft, lev, hd)
                        v.tensor_tensor(inv[:, hd, :, :], xx[:, hd, :, :], four(ident()), ALU.add).then_inc(*step("rw_inv", L, ft, 0, hd))
                        chain(v.tensor_tensor(invT[:, hd, :, :], bm[:, hd, :, 0, :], four(cons[:, K_HG, :]), ALU.mult))
                        v.tensor_tensor(invT[:, hd, :, :], invT[:, hd, :, :], four(ident()), ALU.add).then_inc(*step("rw_invT", L, ft, 0, hd))
                if lev == 0:
                    now("rw_kept", L, ft)
                    continue
                for hd in range(2):
                    if lev < len(RX_LEVELS) - 1:
                        now("rwi_done", L, ft, lev, hd)
                        now("rw_inv", L, ft, lev - 1, hd)
                        b = ps[banks_of.get(("rwi", L, ft, lev, hd), 0)]
                        early = of_tiles(inv[:, hd, :, :], RX_LEVELS[lev], 0)
                        v.tensor_tensor(early, early, bank_halves(b, RX_LEVELS[lev], 0), ALU.add).then_inc(*step("rw_inv", L, ft, lev, hd))
                    now("rwj_done", L, ft, lev, hd)
                    now("rw_invT", L, ft, lev - 1, hd)
                    b = ps[banks_of.get(("rwj", L, ft, lev, hd), 0)]
                    late = of_tiles(invT[:, hd, :, :], RX_LEVELS[lev], 1)
                    v.tensor_tensor(late, late, bank_halves(b, RX_LEVELS[lev], 1), ALU.add).then_inc(*step("rw_invT", L, ft, lev, hd))
                    if lev and hd:
                        next(following, None)
            for _ in range(2):
                next(following, None)
            now("rwq_done", L, ft)
            v.tensor_tensor(q_eff.rearrange("p (t n) -> p t n", n=P), ps[banks_of.get(("rwq", L, ft), 0)][:, :].rearrange("p (t n) -> p t n", n=P), r_dec[:, :, :],
                            ALU.add).then_inc(*step("rw_q", L, ft))
            now("rw_d", L, ft, 1)
            for c in range(NC - 1):
                if c == 0:
                    v.tensor_copy(s_all[:, 1, :], d_mat[:, 0, :]).then_inc(*step("rw_state", L, ft, c))
                else:
                    chain(v.scalar_tensor_tensor(s_pre[:, :], s_all[:, c, :], e_last[:, c:c + 1],
                                                 d_mat[:, c, :], ALU.mult, ALU.add))
                    now("rws_done", L, ft, c)
                    v.tensor_tensor(s_all[:, c + 1, :], s_pre[:, :], ps[banks_of.get(("rws", L, ft, c), 0)][:, 0:HEAD],
                                    ALU.add).then_inc(*step("rw_state", L, ft, c))
                now("rw_state", L, ft, c)
                next(following, None)
            for _ in following:
                pass
            bh = [ps[banks_of.get(("rwy", L, ft, hd), 0)][:, 0:256].rearrange("p (t n) -> p t n", n=HEAD) for hd in range(2)]
            mean = gn_st[:, 0, :, :].rearrange("p t d -> p (t d)")
            for hd in range(2):
                now("rwy_done", L, ft, hd)
                chain(v.tensor_reduce(gn_st[:, 0, :, hd], bh[hd], AX.X, ALU.add))
            chain(v.tensor_scalar(mean, mean, 1.0 / HEAD, None, ALU.mult))
            if ft:
                now("rwo_done", L, ft - 1)
            for hd in range(2):
                v.tensor_tensor(yt[:, 0, :, unit(hd)], bh[hd], gn_st[:, 0, :, hd:hd + 1].to_broadcast([P, NT, HEAD]),
                                ALU.subtract).then_inc(*step("rw_y2", L, ft, hd))

        def by_head(x):
            return x.rearrange("p t (d n) -> p (t d) n", d=2)

        def variance_dve(v, now, chain, L, ft):
            var = gn_st[:, 1, :, :].rearrange("p t d -> p (t d)")
            now("rw_ysq", L, ft)
            chain(v.tensor_reduce(var, by_head(yt[:, 1, :, :]), AX.X, ALU.add))
            v.tensor_scalar(var, var, 1.0 / HEAD, GN_EPS, ALU.mult, ALU.add).then_inc(*step("rw_var", L, ft))

        def gated_dve(v, now, chain, L, ft):
            wide = lambda x: x.rearrange("p t d -> p (t d)").unsqueeze(2).to_broadcast([P, 2 * NT, HEAD])
            row = lambda i: gn_rows[:, i, ft * P:(ft + 1) * P].unsqueeze(1).to_broadcast([P, NT, P])
            y0, y1 = by_head(yt[:, 0, :, :]), by_head(yt[:, 1, :, :])
            now("rw_rstd", L, ft)
            chain(v.tensor_tensor(y0, y0, wide(gn_st[:, 1, :, :]), ALU.mult))
            chain(v.tensor_tensor(yt[:, 0, :, :], yt[:, 0, :, :], row(0), ALU.mult))
            chain(v.tensor_tensor(yt[:, 0, :, :], yt[:, 0, :, :], row(1), ALU.add))
            chain(v.tensor_tensor(y1, by_head(v_tok[:, :, :]), wide(bonus[:, :, :]), ALU.mult))
            chain(v.tensor_tensor(yt[:, 0, :, :], yt[:, 0, :, :], yt[:, 1, :, :], ALU.add))
            now("rwg_done", L, ft)
            v.tensor_tensor(yt[:, 0, :, :], yt[:, 0, :, :], ps[banks_of.get(("rwg", L, ft), 0)][:, :].rearrange("p (t n) -> p t n", n=P),
                            ALU.mult).then_inc(*step("rw_gated", L, ft))

        @block.tensor
        def _(pe):
            order = list(range(8))
            every, dense_banks, core_banks = range(8), range(4), range(4, 8)
            holder = {}
            at_slot = [0]
            at_group = [0]

            def take(key, freed_by, among=every):
                b = next(x for x in order if x in among)
                order.remove(b)
                order.append(b)
                if b in holder:
                    pe.wait_ge(*after(*holder[b]))
                holder[b] = freed_by
                banks_of[key] = b
                return ps[b]

            def used_last(key):
                order.remove(banks_of[key])
                order.append(banks_of[key])

            def dense(name, x, feature_major, freed, own_x=None, among=every, tail=0):
                gname, slots, widths = groups[at_group[0]]
                assert gname == name, (gname, name)
                at_group[0] += 1
                n_tiles = len(widths)
                out_b = []
                n0 = at_slot[0]

                def products(i, kk, m):
                    r, k, ins = (n0 + i) % SPLIT_RING, 2 * i + kk, None
                    if k == 0:
                        out_b.append(take((*name, m), freed(m), among))
                    for xp, wp in ((0, 0), (1, 0), (0, 1)):
                        first = k == 0 and (xp, wp) == (0, 0)
                        last = i == len(slots) - 1 and kk == 1 and (xp, wp) == (0, 1)
                        if feature_major:
                            w = widths[m]
                            o = out_b[m][0:w, :]
                            l_ = w_split[wp][:, r, kk, m * P:m * P + w]
                            r_ = x[xp][:, k, :]
                        else:
                            o = out_b[m][:, :]
                            l_ = x[xp][:, k, m * P:(m + 1) * P]
                            r_ = w_split[wp][:, r, kk, :]
                        ins = nc.tensor.matmul(o, l_, r_, start=first, stop=last)
                        if last:
                            ins.then_inc(*step("dense_done", *name, m))
                        elif wp == 1 and kk == 1 and m == n_tiles - 1:
                            ins.then_inc(*step("w_used", n0 + i))

                for i in range(len(slots)):
                    slot_free[n0 + i] = ("w_used", n0 + i)
                slot_free[n0 + len(slots) - 1] = ("dense_done", *name, n_tiles - 1)
                at_slot[0] += len(slots)
                head = len(slots) - tail
                for i in range(head):
                    pe.wait_ge(*after("w_rest_ready", n0 + i))
                    for kk in range(2):
                        if own_x is not None:
                            own_x(2 * i + kk)
                        for m in range(n_tiles):
                            products(i, kk, m)
                        yield
                for m in range(n_tiles):
                    for i in range(head, len(slots)):
                        if m == 0:
                            pe.wait_ge(*after("w_rest_ready", n0 + i))
                        for kk in range(2):
                            if own_x is not None and m == 0:
                                own_x(2 * i + kk)
                            products(i, kk, m)
                if tail:
                    yield

            def run(g):
                for _ in g:
                    pass

            def advance(g, blocks):
                for _ in range(blocks):
                    next(g, None)

            def to_feature_major(L, q):
                b = {}
                if q < 0:
                    parts = [(range(0, 4), range(NT)), (range(4, 8), range(NT))]
                else:
                    parts = [(range(0, 4), range(NT - 1)), (range(4, 8), range(NT - 1)), (range(8), [NT - 1])]
                for ks, ts in parts:
                    if q < 0:
                        pe.wait_ge(*after(f"x_in{ks[0] // 4}"))
                    for t in ts:
                        if q >= 0 and ks[0] == 0:
                            pe.wait_ge(*after("xn_ready", L, q, t))
                        for k in ks:
                            if t == 0:
                                b[k] = take(("hT", L, q, k), ("hT_raw", L, q, k))
                            ins = nc.tensor.transpose(b[k][:, t * P:(t + 1) * P], h_tok[:, t, k * P:(k + 1) * P], ident())
                            if t == NT - 1:
                                ins.then_inc(*step("hT_done", L, q, k))

            def stream_split(L, q):
                return lambda k: pe.wait_ge(*after("hT_rest", L, q, k))

            def ffn(L, f, q):
                for g in range(FT // 2):
                    run(dense(("up", L, f, g), hT, True,
                              lambda m: ("silu_done", L, f, g, m) if m < 2 else ("act_raw", L, f, g, m - 2),
                              own_x=stream_split(*q) if g == 0 else None))
                if f == 0:
                    pe.wait_ge(*after("par_in", L))
                    b = take(("par", L), ("par_done", L))
                    nc.tensor.transpose(b[:, 0:P], par[:, :], ident()).then_inc(*step("par_T", L))
                else:
                    pe.wait_ge(*after("p_in", L))
                    for k in range(2):
                        b = take(("pT", L, k), ("pT_rest", L, k))
                        for t in range(NT):
                            ins = nc.tensor.transpose(b[:, t * P:(t + 1) * P], p_tok[:, t, k * P:(k + 1) * P], ident())
                        ins.then_inc(*step("pT_done", L, k))

                def arrived(k):
                    pe.wait_ge(*after("act_rest", L, f, k))

                for half in range(2):
                    run(dense(("down", L, f, half), aT, False, lambda m: ("res_sum", L, 2 * f, half, m),
                              own_x=arrived if half == 0 else None, tail=2 * half))

            pe.wait_ge(*after("ident_in"))
            to_feature_major(0, -1)
            for L in range(DEPTH):
                ffn(L, 0, (0, -1) if L == 0 else (L - 1, 3))
                if L == 0:
                    pe.wait_ge(*after("const_in"))
                to_feature_major(L, 0)
                for n in range(3):
                    run(dense(("sb", L, n), hT, n < 2, lambda m: ("sb_in", L, n, m),
                              own_x=stream_split(L, 0) if n == 0 else None))

                def hg_projections():
                    for n in range(4):
                        yield from dense(("hg", L, n), hT, n < 2, lambda m: ("hg_in", L, n, m),
                                         among=dense_banks)

                fill = hg_projections()
                for m in range(4):
                    for n in range(3):
                        pe.wait_ge(*after("sb_in", L, n, m))
                for h in range(4):
                    zb = {}
                    for kb in range(3, -1, -1):
                        zb[kb] = take(("sbz", L, h, kb), ("sb_exp", L, h, kb), core_banks)
                        nc.tensor.matmul(zb[kb][:, kb * P:SEQ], sb_k[:, h, kb * P:(kb + 1) * P], sb_q[:, h, kb * P:SEQ],
                                         start=True, stop=False, skip_group_check=True).then_inc(*step("sbz_done", L, h, kb))
                    advance(fill, 4)
                    for kb in range(3, -1, -1):
                        pe.wait_ge(*after("sb_sp", L, h, kb))
                        for k2 in range(kb, 4):
                            ins = nc.tensor.matmul(zb[kb][:, k2 * P:SEQ], cons[:, K_NTRI if k2 == kb else K_NONE, :],
                                                   sb_sp[:, k2, k2 * P:SEQ], start=False, stop=k2 == 3, skip_group_check=True)
                        ins.then_inc(*step("sb_logit", L, h, kb))
                    advance(fill, 2)
                    o = take(("sby", L, h), ("sb_y", L, h), core_banks)
                    for kb in range(4):
                        pe.wait_ge(*after("sb_att", L, h, kb))
                        ins = nc.tensor.matmul(o[:, kb * P:SEQ], sb_v[:, kb, h * P:(h + 1) * P], sb_att[:, kb, kb * P:SEQ],
                                               start=kb == 0, stop=kb == 3, skip_group_check=True)
                    ins.then_inc(*step("sby_done", L, h))
                    advance(fill, 2)
                run(fill)

                def rwkv_projections():
                    yield from dense(("lora", L), hT, True, lambda m: ("lora_in", L, m), among=dense_banks)
                    yield from dense(("rkv", L, 0), hT, True, lambda m: ("rkv_in", L, 0, m), among=dense_banks)

                fill = rwkv_projections()
                pe.wait_ge(*after("hg_kx", L))
                for lev in range(-1, len(HG_LEVELS)):
                    if lev >= 0:
                        pe.wait_ge(*after("hg_K", L, lev))
                    for t in range(NT):
                        b = take(("hga", L, lev, t), ("hg_att", L, lev, t), core_banks)
                        for h in range(4):
                            tok = slice(t * P, (t + 1) * P)
                            kk_, qq_ = (hg_k, hg_q) if lev < 0 else (hg_K, hg_Q)
                            ins = nc.tensor.matmul(b[:, h * P:(h + 1) * P], kk_[:, h, tok], qq_[:, h, tok], start=True, stop=True)
                        ins.then_inc(*step("hga_done", L, lev, t))
                    if lev < 6:
                        advance(fill, 2)
                run(fill)

                def later_projections():
                    for ft in range(1, 4):
                        yield from dense(("rkv", L, ft), hT, True, lambda m: ("rkv_in", L, ft, m), among=range(3))
                    yield from dense(("gate", L, 0, 0), hT, True, lambda m: ("gate_sig", L, 0, 0, m), among=dense_banks)

                fill = later_projections()
                pe.wait_ge(*after("hg_K", L, 99))
                for t in range(NT):
                    b = take(("hgk", L, t), ("hg_ktok", L, t), core_banks)
                    for h in range(4):
                        ins = nc.tensor.transpose(b[:, h * P:(h + 1) * P], hg_K[:, h, t * P:(t + 1) * P], ident())
                    ins.then_inc(*step("hgk_done", L, t))
                advance(fill, 1)
                for t in range(NT - 1):
                    pe.wait_ge(*after("hg_ktok", L, t))
                    b = take(("hgd", L, t), ("hg_state", L, t, 3), core_banks)
                    for h in range(4):
                        ins = nc.tensor.matmul(b[:, h * P:(h + 1) * P], hg_p[:, t, h * P:(h + 1) * P],
                                               hg_v[:, t, h * P:(h + 1) * P], start=True, stop=True)
                    ins.then_inc(*step("hgd_done", L, t))
                    if t < 2:
                        advance(fill, 1)
                for t in range(NT):
                    b = take(("hgo", L, t), ("hg_o", L, t), core_banks)
                    pe.wait_ge(*after("hg_att", L, len(HG_LEVELS) - 1, t))
                    if t:
                        pe.wait_ge(*after("hg_state", L, t - 1, 3))
                    for h in range(4):
                        ins = nc.tensor.matmul(b[:, h * P:(h + 1) * P], hg_att[:, t, h, :], hg_v[:, t, h * P:(h + 1) * P],
                                               start=True, stop=t == 0)
                        if t:
                            ins = nc.tensor.matmul(b[:, h * P:(h + 1) * P], hg_Q[:, h, t * P:(t + 1) * P],
                                                   hg_S[:, t, h, :], start=False, stop=True)
                    ins.then_inc(*step("hgo_done", L, t))
                rates_pe(pe, take, L, 0)
                advance(fill, 2)
                for t in range(NT):
                    pe.wait_ge(*after("hg_ytok", L, t))
                    b = take(("hgt", L, t), ("hg_y", L, t), core_banks)
                    for h in range(4):
                        ins = nc.tensor.transpose(b[:, h * P:(h + 1) * P], hg_o_buf(t)[:, h * P:(h + 1) * P], ident())
                    ins.then_inc(*step("hgt_done", L, t))

                advance(fill, 2)
                key_norms_pe(pe, take, L, 0)
                advance(fill, 1)
                for ft in range(4):
                    rwkv_core_pe(pe, take, used_last, lambda n: advance(fill, n), L, ft)
                output_gate_pe(pe, take, L, 3)
                run(fill)
                output_pe(pe, take, L, 3)
                for half in range(2):
                    for br in range(3):
                        if half or br:
                            run(dense(("gate", L, half, br), hT, True, lambda m: ("gate_sig", L, half, br, m)))
                        run(dense(("branch", L, half, br), yT, True, lambda m: ("merge", L, half, br, m),
                                  own_x=lambda k: pe.wait_ge(*after("yT_rest", L, half, br, k))))

                def merged(k):
                    pe.wait_ge(*after("mT_rest", L, k))

                for half in range(2):
                    run(dense(("out", L, half), mT, False, lambda m: ("res_sum", L, 1, half, m),
                              own_x=merged if half == 0 else None, tail=2 * half))
                to_feature_major(L, 1)
                ffn(L, 1, (L, 1))
                to_feature_major(L, 2)
                for k in range(2):
                    pe.wait_ge(*after("pT_rest", L, k))
                for half in range(2):
                    run(dense(("pgate", L, half), hT, False, lambda m: ("ple_sig", L, half, m),
                              own_x=stream_split(L, 2) if half == 0 else None))
                    run(dense(("pproj", L, half), pT, False, lambda m: ("ple_mul", L, half, m), tail=1))
                if L < DEPTH - 1:
                    to_feature_major(L, 3)

        @block.gpsimd
        def _(pool):
            nc.gpsimd.memset(zero[:, :], 0.0).then_inc(*step("zero_set"))
            pool.wait_ge(*after("zero_set"))
            for n, (pieces, g, i) in enumerate(slot_list):
                r, q = n % RAW_RING, n % SPLIT_RING
                w = sum(x[2] for x in pieces)
                pool.wait_ge(*after(f"w_in{r}", n))
                if n >= SPLIT_RING:
                    pool.wait_ge(*after(*slot_free[n - SPLIT_RING]))
                nc.gpsimd.tensor_tensor(w_split[0][:, q, :, 0:w], w_raw[:, r, :, 0:w],
                                        zero[:, 0:1].unsqueeze(2).to_broadcast([P, 2, w]), ALU.add).then_inc(*step("w_high", n))
                pool.wait_ge(*after("w_high", n))
                nc.gpsimd.tensor_tensor(w_split[1][:, q, :, 0:w], w_raw[:, r, :, 0:w],
                                        w_split[0][:, q, :, 0:w].bitcast(F32), ALU.subtract).then_inc(*step("w_rest_ready", n))

        @block.sync
        def _(sp):
            x_t = a["x"][0].rearrange("(t p) d -> p t d", p=P)
            flat = cons[:, :, :].rearrange("p a n -> p (a n)")
            sp.dma_start(flat[:, 0:P], a["consts"][:, 0:P]).then_inc(*step("ident_in", by=16))
            for half in range(2):
                cols = slice(512 * half, 512 * half + 512)
                sp.dma_start(h_tok[:, :, cols], x_t[:, :, cols]).then_inc(*step(f"x_in{half}", by=16))

            def load_weights(upto):
                while done[0] < min(upto, len(slot_list)):
                    n = done[0]
                    done[0] += 1
                    pieces, g, i = slot_list[n]
                    r = n % RAW_RING
                    if n >= RAW_RING:
                        sp.wait_ge(*after("w_rest_ready", n - RAW_RING))
                    for src, at, w in pieces:
                        sp.dma_start(w_raw[:, r, :, at:at + w], src).then_inc(*step(f"w_in{r}", n, by=16))

            done = [0]
            load_weights(RAW_RING)
            sp.dma_start(flat[:, P:], a["consts"][:, P:]).then_inc(*step("const_in", by=16))
            load_weights(len(slot_list))

        @block.scalar
        def _(act):
            def chain(ins):
                ins.then_inc(*step("act_chain"))
                act.wait_ge(*after("act_chain"))

            def now(name, *index):
                act.wait_ge(*after(name, *index))

            def load_params(L):
                if L:
                    now("par_done", L - 1)
                rows = [(R_LNG, a["ln_g"][L].rearrange("q (k p) -> (q k) p", p=P), 32),
                        (R_LNB, a["ln_b"][L].rearrange("q (k p) -> (q k) p", p=P), 32),
                        (R_MU, a["rw_mu"][L, 0:14 * P].rearrange("(k p) -> k p", p=P), 14)]
                for row, key in ((R_W0, "rw_w0"), (R_A0, "rw_a0"), (R_KK, "rw_k_k"), (R_KA, "rw_k_a")):
                    rows.append((row, a[key][L].rearrange("(k p) -> k p", p=P), 4))
                rows.append((R_RK, a["rw_r_k"][L].rearrange("(k h) n -> k (h n)", h=2), 4))
                rows.append((R_LB, a["hg_lb_raw"].rearrange("l (k p) -> (l k) p", p=P), 8))
                for row, src, n in rows:
                    act.dma_start(par[row:row + n, :], src).then_inc(*step("par_in", L, by=16))
                act.dma_start(par[R_MU + 14:R_MU + 15, 0:32], a["rw_mu"][L:L + 1, 14 * P:14 * P + 32]).then_inc(*step("par_in", L, by=16))

            def param_columns(L):
                now("par_T", L)
                if L:
                    now("hT_raw", L - 1, 3, KD - 1)
                nc.scalar.activation(parT[:, :], ps[banks_of.get(("par", L), 0)][:, 0:P], ACT.Copy).then_inc(*step("par_done", L))
                now("par_done", L)

            def feature_major(L, q, scale):
                for k in range(KD):
                    b = ps[banks_of.get(("hT", L, q, k), 0)]
                    now("hT_done", L, q, k)
                    if scale:
                        g = parT[:, R_LNG + 8 * q + k:R_LNG + 8 * q + k + 1]
                        o = parT[:, R_LNB + 8 * q + k:R_LNB + 8 * q + k + 1]
                        nc.scalar.activation(h_raw[:, k, :], b[:, :], ACT.Identity, bias=o, scale=g).then_inc(
                            *step("hT_raw", L, q, k))
                    else:
                        nc.scalar.activation(h_raw[:, k, :], b[:, :], ACT.Copy).then_inc(*step("hT_raw", L, q, k))

            def norm(L, q, last=False):
                for t in range(NT):
                    now("ln_var", L, q, t)
                    nc.scalar.activation(ln_rstd[:, t, :], ln_mv[:, t, 1:2], ACT.Sqrt, bias=ln_eps[:, :]).then_inc(*step("ln_sqrt", L, q, t))
                now(*{0: ("dense_done", "down", L, 0, 1, 3), 1: ("dense_done", "out", L, 1, 3),
                      2: ("dense_done", "down", L, 1, 1, 3), 3: ("h_scaled", L, 2, NT - 1)}[q])
                act.dma_start(ln_rows[:, 0, :], a["ln_g"][L, q:q + 1, :].partition_broadcast(P)).then_inc(*step("rows_in", L, q, by=16))
                act.dma_start(ln_rows[:, 1, :], a["ln_b"][L, q:q + 1, :].partition_broadcast(P)).then_inc(*step("rows_in", L, q, by=16))
                if q == 1:
                    act.dma_start(p_tok[:, :, :], a["p"][L, 0].rearrange("(t p) d -> p t d", p=P)).then_inc(*step("p_in", L, by=16))
                if not last:
                    feature_major(L, q, True)

            def ffn(L, f):
                for g in range(FT // 2):
                    for m in range(2):
                        now("dense_done", "up", L, f, g, m)
                        if g:
                            now("act_raw", L, f, g - 1, m)
                        b = ps[banks_of.get(("up", L, f, g, m), 0)]
                        nc.scalar.activation(silu[:, m, :], b[:, :], ACT.Silu).then_inc(*step("silu_done", L, f, g, m))
                if f == 0:
                    param_columns(L)
                    if L + 1 < DEPTH:
                        load_params(L + 1)
                else:
                    for k in range(2):
                        now("pT_done", L, k)
                        nc.scalar.activation(pT[0][:, k, :], ps[banks_of.get(("pT", L, k), 0)][:, :], ACT.Copy).then_inc(
                            *step("pT_high", L, k))

            def hgrn_inputs(L, n):
                def bank(m):
                    now("dense_done", "hg", L, n, m)
                    return ps[banks_of.get(("hg", L, n, m), 0)]

                if n == 0:
                    for m in range(4):
                        nc.scalar.activation(hg_q[:, m, :], bank(m)[:, :], ACT.Sigmoid).then_inc(*step("hg_in", L, 0, m))
                if n == 1:
                    for m in range(4):
                        nc.scalar.activation(hg_k[:, m, :], bank(m)[:, :], ACT.Copy).then_inc(*step("hg_in", L, 1, m))
                if n == 2:
                    for m in range(4):
                        nc.scalar.activation(hg_v[:, m, :], bank(m)[:, :], ACT.Copy).then_inc(*step("hg_in", L, 2, m))
                if n == 3:
                    for m in range(4):
                        nc.scalar.activation(hg_g[:, m, :], bank(m)[:, :], ACT.Silu).then_inc(*step("hg_in", L, 3, m))

            def forget_logs(L, second):
                e = hg_e[:, :, :].rearrange("p a n -> p (a n)")
                src = hg_k
                if second:
                    now("hg_bf", L, 3)
                    src = hg_x
                else:
                    now("hg_in", L, 1, 3)
                chain(nc.scalar.activation(e, src[:, :, :].rearrange("p m n -> p (m n)"), ACT.Abs))
                chain(nc.scalar.activation(e, e, ACT.Exp, scale=-1.0))
                if second:
                    nc.scalar.activation(hg_k[:, :, :], hg_k[:, :, :], ACT.Exp).then_inc(*step("hg_kx", L))
                nc.scalar.activation(e, e, ACT.Ln, bias=1.0).then_inc(*step("hg_ln2" if second else "hg_ln1", L))

            def lora_inputs(L):
                for m in range(3):
                    w = (P, P, 32)[m]
                    now("dense_done", "lora", L, m)
                    if m == 0:
                        now("rw_u0", L)
                    nc.scalar.activation(rw_u[0:w, m, 1:SEQ + 1], ps[banks_of.get(("lora", L, m), 0)][0:w, :], ACT.Copy).then_inc(
                        *step("lora_in", L, m))

            def rkv_inputs(L, ft):
                for m in range(3):
                    now("dense_done", "rkv", L, ft, m)
                    if ft:
                        now("rkv_mix", L, ft - 1, m)
                    else:
                        now("lora_mix", L, m)
                    nc.scalar.activation(rw_u[:, m, 1:SEQ + 1], ps[banks_of.get(("rkv", L, ft, m), 0)][:, :], ACT.Copy).then_inc(
                        *step("rkv_in", L, ft, m))

            def rates(L, ft):
                now("rww_done", L, ft)
                if ft:
                    now("rw_kd", L, ft - 1)
                nc.scalar.activation(rw_sw[:, :], ps[banks_of.get(("rww", L, ft), 0)][:, :], ACT.Sigmoid,
                                     bias=parT[:, R_W0 + ft:R_W0 + ft + 1]).then_inc(*step("rw_sw", L, ft))
                now("rwa_done", L, ft)
                nc.scalar.activation(rw_a[:, :], ps[banks_of.get(("rwa", L, ft), 0)][:, :], ACT.Sigmoid,
                                     bias=parT[:, R_A0 + ft:R_A0 + ft + 1]).then_inc(*step("rw_a", L, ft))

            def norms(L, ft):
                now("rw_kkr", L, ft)
                nc.scalar.activation(rw_ss[:, :], rw_kk[:, :], ACT.Square).then_inc(*step("rw_sq", L, ft))
                now("rw_csm", L, ft)
                if ft:
                    now("rw_kept", L, ft - 1)
                nc.scalar.activation(rw_e1[:, :], rw_cs[:, :], ACT.Exp, scale=-DECAY).then_inc(*step("rw_e1", L, ft))
                now("rw_e1", L, ft)
                nc.scalar.activation(rw_cs[:, :], rw_cs[:, :], ACT.Exp, scale=DECAY).then_inc(*step("rw_e2", L, ft))
                nc.scalar.activation(rw_e3[:, :], rw_e3[:, :], ACT.Exp, scale=-DECAY).then_inc(*step("rw_e3", L, ft))
                now("rw_ssmax", L, ft)
                chain(nc.scalar.activation(rw_ss[:, :], rw_ss[:, :], ACT.Ln, scale=SS_SCALE))
                nc.scalar.activation(rw_ss[:, :], rw_ss[:, :], ACT.Exp, scale=-0.5).then_inc(*step("rw_rn", L, ft))

            def token_major(L, ft, i):
                now("rwt_done", L, ft, i)
                b = ps[banks_of.get(("rwt", L, ft, i), 0)]
                if i == 1:
                    src = b[:, :].rearrange("p (t d n) -> p t d n", t=NT, d=2)
                    if ft:
                        now("rwy_done", L, ft - 1, 1)
                    for hd in range(2):
                        ins = nc.scalar.activation(rhs[:, hd, :, 0:HEAD], src[:, :, hd, :], ACT.Copy)
                else:
                    dst = {0: v_tok, 2: b_tok, 3: k_tok}[i]
                    ins = nc.scalar.activation(dst[:, :, :].rearrange("p t n -> p (t n)"), b[:, :], ACT.Copy)
                ins.then_inc(*step("rw_tok", L, ft, i))

            def squares(L, ft):
                now("rw_y2", L, ft, 1)
                nc.scalar.activation(yt[:, 1, :, :], yt[:, 0, :, :], ACT.Square).then_inc(*step("rw_ysq", L, ft))

            def deviation(L, ft):
                now("rw_var", L, ft)
                chain(nc.scalar.activation(gn_st[:, 1, :, :], gn_st[:, 1, :, :], ACT.Ln))
                nc.scalar.activation(gn_st[:, 1, :, :], gn_st[:, 1, :, :], ACT.Exp, scale=-0.5).then_inc(*step("rw_rstd", L, ft))

            def output(L, ft):
                now("rwo_done", L, ft)
                nc.scalar.activation(y_raw[:, 2, ft, :], ps[banks_of.get(("rwo", L, ft), 0)][:, :], ACT.Copy).then_inc(
                    *step("rw_yT", L, ft))

            now("par_zero")
            load_params(0)
            feature_major(0, -1, False)
            for L in range(DEPTH):
                ffn(L, 0)
                norm(L, 0)

                for t in range(NT):
                    now("h_scaled", L, 0, t)
                    act.dma_start(h_dram[t, :, :], h_tok[:, t, :]).then_inc(*step("h_out", L, by=16))
                now("h_out", L)
                if L:
                    now("lb_abs", L)
                    chain(nc.scalar.activation(lbT[:, 12:16], lbT[:, 12:16], ACT.Exp, scale=-1.0))
                    nc.scalar.activation(lbT[:, 12:16], lbT[:, 12:16], ACT.Ln, bias=1.0).then_inc(*step("lb_ln", L))
                for n in range(3):
                    dst = (sb_q, sb_k, sb_v)[n]
                    for m in range(4):
                        now("dense_done", "sb", L, n, m)
                        b = ps[banks_of.get(("sb", L, n, m), 0)]
                        nc.scalar.activation(dst[:, m, :], b[:, :], ACT.Copy, scale=P ** -0.5 if n == 0 else 1.0).then_inc(
                            *step("sb_in", L, n, m))
                for h in range(4):
                    for kb in range(3, -1, -1):
                        now("sbz_done", L, h, kb)
                        if h:
                            now("sb_sp0", L, h - 1, kb)
                        nc.scalar.activation(sb_e[:, kb, kb * P:SEQ], ps[banks_of.get(("sbz", L, h, kb), 0)][:, kb * P:SEQ],
                                             ACT.Abs).then_inc(*step("sb_abs", L, h, kb))
                    for kb in range(3, -1, -1):
                        now("sb_abs", L, h, kb)
                        nc.scalar.activation(sb_e[:, kb, kb * P:SEQ], sb_e[:, kb, kb * P:SEQ], ACT.Exp, scale=-1.0).then_inc(
                            *step("sb_expabs", L, h, kb))
                    for kb in range(3, -1, -1):
                        now("sb_expabs", L, h, kb)
                        nc.scalar.activation(sb_e[:, kb, kb * P:SEQ], sb_e[:, kb, kb * P:SEQ], ACT.Ln, bias=1.0).then_inc(
                            *step("sb_ln", L, h, kb))
                    if h >= 2:
                        forget_logs(L, h == 3)
                    for kb in range(3, -1, -1):
                        b = ps[banks_of.get(("sbz", L, h, kb), 0)]
                        cols = slice(kb * P, SEQ)
                        now("sb_logit", L, h, kb)
                        if h:
                            now("sby_done", L, h - 1)
                        nc.scalar.activation(sb_att[:, kb, cols], b[:, cols], ACT.Exp).then_inc(*step("sb_exp", L, h, kb))
                    now("sby_done", L, h)
                    nc.scalar.activation(y_raw[:, 0, h, :], ps[banks_of.get(("sby", L, h), 0)][:, :], ACT.Copy).then_inc(
                        *step("sb_y", L, h))
                    hgrn_inputs(L, h)

                now("sby_done", L, 3)
                nc.scalar.activation(hg_Q[:, :, :], hg_q[:, :, :], ACT.Copy).then_inc(*step("hg_Q0", L))
                act.dma_start(hg_row[:, :], a["hg_norm_g"][L:L + 1, :].partition_broadcast(P)).then_inc(*step("hg_row_in", L, by=16))
                for lev in range(len(HG_LEVELS)):
                    hgt, n = HG_LEVELS[lev], 2048 // (2 * HG_LEVELS[lev])
                    if lev == 0:
                        for m in range(4):
                            now("hg_lf", L, m)
                    else:
                        now("hg_pupd", L, lev - 1)
                    if lev >= 2:
                        now("hg_K", L, lev - 2)
                    view = lambda t_: t_[:, :, :].rearrange("p h (n two s) -> p (h n) two s", two=2, s=hgt)
                    e0, e1 = [hg_decay(lev, i).rearrange("p (n s) -> p n s", s=hgt) for i in range(2)]
                    nc.scalar.activation(e0, view(hg_p)[:, :, 1, :], ACT.Exp).then_inc(*step("hg_ep", L, lev))
                    if lev:
                        nc.scalar.activation(e1, view(hg_x)[:, :, 0, :], ACT.Exp).then_inc(*step("hg_ex", L, lev))
                    if lev == 4:
                        lora_inputs(L)
                now("hg_pupd", L, len(HG_LEVELS) - 1)
                nc.scalar.activation(hg_p[:, :, :], hg_p[:, :, :], ACT.Exp).then_inc(*step("hg_expP", L))
                nc.scalar.activation(hg_x[:, :, :], hg_x[:, :, :], ACT.Exp).then_inc(*step("hg_expX", L))
                now("hg_K", L, 99)
                now("hg_glast", L)
                for t in range(NT):
                    now("hgk_done", L, t)
                    nc.scalar.activation(hg_p[:, t, :], ps[banks_of.get(("hgk", L, t), 0)][:, :], ACT.Copy).then_inc(
                        *step("hg_ktok", L, t))
                rkv_inputs(L, 0)
                act.dma_start(w_up[0:64, :], a["rw_w_up"][L]).then_inc(*step("rw_wts", L, by=16))
                act.dma_start(w_up[64:128, :], a["rw_a_up"][L]).then_inc(*step("rw_wts", L, by=16))
                act.dma_start(g_up[:, 0, :], a["rw_g_up"][L, 0:128, :]).then_inc(*step("rw_wts", L, by=16))
                act.dma_start(g_up[0:32, 1, :], a["rw_g_up"][L, 128:160, :]).then_inc(*step("rw_wts", L, by=16))
                act.dma_start(gn_rows[:, 0, :], a["rw_gn_g"][L:L + 1, :].partition_broadcast(P)).then_inc(*step("rw_wts", L, by=16))
                act.dma_start(gn_rows[:, 1, :], a["rw_gn_b"][L:L + 1, :].partition_broadcast(P)).then_inc(*step("rw_wts", L, by=16))
                now("lora_mix", L, 0)
                nc.scalar.activation(lora_x[0:64, 0, :], lora_x[0:64, 0, :], ACT.Tanh).then_inc(*step("lora_act", L, 0))
                now("lora_mix", L, 2)
                nc.scalar.activation(lora_x[:, 1, :], lora_x[:, 1, :], ACT.Sigmoid).then_inc(*step("lora_act", L, 1))
                nc.scalar.activation(lora_x[0:32, 2, :], lora_x[0:32, 2, :], ACT.Sigmoid).then_inc(*step("lora_act", L))
                for t in range(NT):
                    now("hgo_done", L, t)
                    if t >= 2:
                        now("hg_ms", L, t - 2)
                    nc.scalar.activation(hg_e[:, t % 2, 0:512], ps[banks_of.get(("hgo", L, t), 0)][:, :], ACT.Square).then_inc(
                        *step("hg_osq", L, t))
                for t in range(NT):
                    now("hg_ms", L, t)
                nc.scalar.activation(gn_small("hg_r"), gn_small("hg_r"), ACT.Sqrt, scale=1.0 / P).then_inc(*step("hg_sqrt", L))
                rates(L, 0)
                for t in range(NT):
                    now("hgt_done", L, t)
                    nc.scalar.activation(y_raw[:, 1, :, t * P:(t + 1) * P],
                                         ps[banks_of.get(("hgt", L, t), 0)][:, :].rearrange("p (h n) -> p h n", h=4),
                                         ACT.Copy).then_inc(*step("hg_y", L, t))

                norms(L, 0)
                rkv_inputs(L, 1)
                for ft in range(4):
                    if ft:
                        squares(L, ft - 1)
                    token_major(L, ft, 2)
                    token_major(L, ft, 3)
                    token_major(L, ft, 1)
                    if ft:
                        deviation(L, ft - 1)
                        now("rw_gated", L, ft - 1)
                    token_major(L, ft, 0)
                    if ft:
                        output(L, ft - 1)
                    if ft < 3:
                        rates(L, ft + 1)
                        norms(L, ft + 1)
                    now("rwl_done", L, ft)
                    nc.scalar.activation(rhs[:, :, :, HEAD:P].rearrange("p d t n -> p (d t) n"),
                                         ps[banks_of.get(("rwl", L, ft), 0)][:, :].rearrange("p (u n) -> p u n", n=HEAD),
                                         ACT.Copy).then_inc(*step("rw_lakv", L, ft))
                    for hd in range(2):
                        now("rwu_done", L, ft, hd)
                        nc.scalar.activation(xx[:, hd, :, :].rearrange("p t n -> p (t n)"),
                                             ps[banks_of.get(("rwu", L, ft, hd), 0)][:, :], ACT.Copy).then_inc(*step("rw_wu", L, ft, hd))
                    for name, dst in (("p", p_mat), ("d", d_mat)):
                        for cp in range(2):
                            now(f"rw{name}_done", L, ft, cp)
                            nc.scalar.activation(dst.rearrange("p (t two) n -> p t two n", two=2)[:, :, cp, :],
                                                 ps[banks_of.get((f"rw{name}", L, ft, cp), 0)][:, 0:256].rearrange("p (t n) -> p t n", n=HEAD),
                                                 ACT.Copy).then_inc(*step(f"rw_{name}", L, ft, cp))
                    if ft < 2:
                        rkv_inputs(L, ft + 2)
                squares(L, 3)
                deviation(L, 3)
                output(L, 3)

                now("rw_yT", L, 3)
                for half in range(2):
                    for br in range(3):
                        for m in range(4):
                            now("dense_done", "gate", L, half, br, m)
                            if half or br:
                                now("merge", L, *divmod(3 * half + br - 1, 3), m)
                            nc.scalar.activation(gate_s[:, m, :], ps[banks_of.get(("gate", L, half, br, m), 0)][:, :],
                                                 ACT.Sigmoid).then_inc(*step("gate_sig", L, half, br, m))
                now("yT_rest", L, 1, 2, 3)
                for t in range(NT):
                    act.dma_start(h_tok[:, t, :], h_dram[t, :, :]).then_inc(*step("h_back", L, by=16))
                norm(L, 1)
                ffn(L, 1)
                norm(L, 2)
                for half in range(2):
                    for m in range(4):
                        now("dense_done", "pgate", L, half, m)
                        if half:
                            now("ple_mul", L, 0, m)
                        nc.scalar.activation(ple_sig[:, m, :], ps[banks_of.get(("pgate", L, half, m), 0)][:, :], ACT.Sigmoid).then_inc(
                            *step("ple_sig", L, half, m))
                norm(L, 3, last=L == DEPTH - 1)
            for t in range(NT):
                now("h_final", t)
                act.dma_start(out[0, t * P:(t + 1) * P, :], h_new[:, t % 2, :]).then_inc(*step(f"stored{t % 2}", t, by=16))
            now("stored0", NT - 2)
            now("stored1", NT - 1)

        @block.vector
        def _(dve):
            def chain(ins):
                ins.then_inc(*step("dve_chain"))
                dve.wait_ge(*after("dve_chain"))

            def now(name, *index):
                dve.wait_ge(*after(name, *index))

            v = nc.vector

            def split(L, q):
                for k in range(KD):
                    now("hT_raw", L, q, k)
                    chain(v.tensor_copy(hT[0][:, k, :], h_raw[:, k, :]))
                    v.tensor_tensor(hT[1][:, k, :], h_raw[:, k, :], hT[0][:, k, :].bitcast(F32), ALU.subtract).then_inc(
                        *step("hT_rest", L, q, k))

            def stats(L, q, t, half):
                now("res_sum", L, q, half, t)
                v.bn_stats(ln_small[:, t, 6 * half:6 * half + 6], h_tok[:, t, 512 * half:512 * half + 512]).then_inc(
                    *step("bn_done", L, q, t, half))

            def normalise(L, q, t):
                stats(L, q, t, 1)
                now("bn_done", L, q, t, 1)
                v.bn_aggr(ln_mv[:, t, :], ln_small[:, t, 0:12]).then_inc(*step("ln_var", L, q, t))
                now("ln_sqrt", L, q, t)
                chain(v.reciprocal(ln_rstd[:, t, :], ln_rstd[:, t, :]))
                v.tensor_scalar(h_tok[:, t, :], h_tok[:, t, :], ln_mv[:, t, 0:1], ln_rstd[:, t, :], ALU.subtract, ALU.mult).then_inc(
                    *step("xn_ready", L, q, t))

            def norm(L, q, last=False):
                if last:
                    now("rows_in", L, q)
                    for t in range(NT):
                        now("xn_ready", L, q, t)
                        if t >= 2:
                            now(f"stored{t % 2}", t - 2)
                        chain(v.tensor_tensor(h_new[:, t % 2, :], h_tok[:, t, :], ln_rows[:, 0, :], ALU.mult))
                        v.tensor_tensor(h_new[:, t % 2, :], h_new[:, t % 2, :], ln_rows[:, 1, :], ALU.add).then_inc(*step("h_final", t))
                    return
                split(L, q)
                now("rows_in", L, q)
                chain(v.tensor_scalar(ln_rows[:, :, :], ln_rows[:, :, :], ALPHA, None, ALU.mult))
                now("hT_done", L, q, KD - 1)
                for t in range(NT):
                    chain(v.tensor_tensor(h_tok[:, t, :], h_tok[:, t, :], ln_rows[:, 0, :], ALU.mult))
                    v.tensor_tensor(h_tok[:, t, :], h_tok[:, t, :], ln_rows[:, 1, :], ALU.add).then_inc(*step("h_scaled", L, q, t))

            def ffn(L, f):
                for g in range(FT // 2):
                    for m in range(2):
                        now("silu_done", L, f, g, m)
                        now("dense_done", "up", L, f, g, m + 2)
                        b = ps[banks_of.get(("up", L, f, g, m + 2), 0)]
                        v.tensor_tensor(act_raw[:, m, :], silu[:, m, :], b[:, :], ALU.mult).then_inc(*step("act_raw", L, f, g, m))
                        now("act_raw", L, f, g, m)
                        k = 2 * g + m
                        chain(v.tensor_copy(aT[0][:, k, :], act_raw[:, m, :]))
                        v.tensor_tensor(aT[1][:, k, :], act_raw[:, m, :], aT[0][:, k, :].bitcast(F32), ALU.subtract).then_inc(
                            *step("act_rest", L, f, k))
                if f == 1:
                    for k in range(2):
                        now("pT_high", L, k)
                        v.tensor_tensor(pT[1][:, k, :], ps[banks_of.get(("pT", L, k), 0)][:, :], pT[0][:, k, :].bitcast(F32),
                                        ALU.subtract).then_inc(*step("pT_rest", L, k))
                residual("down", L, 2 * f, (f,))

            def residual(name, L, q, extra):
                for half in range(2):
                    for m in range(4):
                        now("dense_done", name, L, *extra, half, m)
                        b = ps[banks_of.get((name, L, *extra, half, m), 0)]
                        z = h_tok[:, m, 512 * half:512 * half + 512]
                        v.scalar_tensor_tensor(z, b[:, :], 0.5 if name == "down" else 1.0, z, ALU.mult, ALU.add).then_inc(
                            *step("res_sum", L, q, half, m))
                        if half:
                            normalise(L, q, m)
                        else:
                            stats(L, q, m, 0)

            def lora_mix(L):
                for m in range(3):
                    w = (P, P, 32)[m]
                    now("lora_in", L, m)
                    if m:
                        now("lora_mix", L, m - 1)
                    shift_mix(v, chain, rw_u[0:w, m, :], rw_d[0:w, :], lora_x[0:w, m, :], parT[0:w, R_MU + 12 + m:R_MU + 13 + m]).then_inc(
                        *step("lora_mix", L, m))

            def forget_gate(L):
                e = hg_e[:, :, :].rearrange("p a (b n) -> p (a b) n", n=SEQ)
                now("hg_ln1", L)
                chain(v.scalar_tensor_tensor(hg_p[:, :, :], hg_k[:, :, :], 0.0, e, ALU.min, ALU.subtract))
                for m in range(4):
                    chain(v.tensor_scalar(hg_p[:, m, :], hg_p[:, m, :], lbT[:, 4 + m:5 + m], None, ALU.add))
                    v.tensor_scalar(hg_x[:, m, :], hg_p[:, m, :], lbT[:, m:m + 1], None, ALU.subtract)
                    v.tensor_tensor(hg_k[:, m, :], hg_p[:, m, :], hg_k[:, m, :], ALU.subtract).then_inc(*step("hg_bf", L, m))

            def forget_rate(L):
                now("hg_ln2", L)
                for m in range(4):
                    now("hg_bf", L, m)
                    v.scalar_tensor_tensor(hg_p[:, m, :], hg_p[:, m, :], lbT[:, m:m + 1],
                                           hg_e[:, m // 2, SEQ * (m % 2):SEQ * (m % 2) + SEQ], ALU.max, ALU.add).then_inc(
                        *step("hg_lf", L, m))
                chain(v.memset(hg_x[:, :, :], 0.0))

            v.memset(ln_eps[:, :], LN_EPS)
            v.memset(par[:, :], 0.0).then_inc(*step("par_zero"))
            split(0, -1)
            now("hT_done", 0, -1, KD - 1)
            chain(v.tensor_scalar(h_tok[:, :, :], h_tok[:, :, :], ALPHA, None, ALU.mult))
            for L in range(DEPTH):
                ffn(L, 0)
                norm(L, 0)
                now("par_done", L)
                lb_log, lb_rest, lb_s = lbT[:, 0:4], lbT[:, 4:8], lbT[:, 8:12]
                if L == 0:
                    v.memset(lb_log, LOG_ZERO)
                    v.memset(lb_rest, 0.0).then_inc(*step("lb_set", L))
                else:
                    chain(v.tensor_tensor(lb_s, parT[:, R_LB + 4:R_LB + 8], parT[:, R_LB:R_LB + 4], ALU.subtract))
                    v.scalar_tensor_tensor(lbT[:, 12:16], lb_s, -1.0, lb_s, ALU.mult, ALU.max).then_inc(*step("lb_abs", L))
                    now("lb_ln", L)
                    chain(v.scalar_tensor_tensor(lb_rest, lb_s, 0.0, lbT[:, 12:16], ALU.max, ALU.add))
                    chain(v.tensor_tensor(lb_log, lb_s, lb_rest, ALU.subtract))
                    v.tensor_scalar(lb_rest, lb_rest, -1.0, None, ALU.mult).then_inc(*step("lb_set", L))
                now("lb_set", L)
                for h in range(4):
                    for kb in range(3, -1, -1):
                        b = ps[banks_of.get(("sbz", L, h, kb), 0)]
                        cols = slice(kb * P, SEQ)
                        diag = slice(kb * P, kb * P + P)
                        now("sb_ln", L, h, kb)
                        if h:
                            now("sb_logit", L, h - 1, 0)
                        v.scalar_tensor_tensor(sb_sp[:, kb, cols], b[:, cols], 0.0, sb_e[:, kb, cols], ALU.max, ALU.add).then_inc(
                            *step("sb_sp0", L, h, kb))
                        now("sb_sp0", L, h, kb)
                        v.tensor_tensor(sb_sp[:, kb, diag], sb_sp[:, kb, diag], cons[:, K_CAUSAL, :], ALU.mult).then_inc(
                            *step("sb_sp", L, h, kb))
                    if h == 2:
                        forget_gate(L)
                    if h == 3:
                        forget_rate(L)
                    for kb in range(3, -1, -1):
                        diag = slice(kb * P, kb * P + P)
                        now("sb_exp", L, h, kb)
                        v.scalar_tensor_tensor(sb_att[:, kb, diag], sb_att[:, kb, diag], 3e38, cons[:, K_CAUSAL, :], ALU.min,
                                               ALU.mult).then_inc(*step("sb_att", L, h, kb))
                now("sb_y", L, 3)
                now("hg_Q0", L)
                now("hg_lf", L, 3)
                now("hg_kx", L)
                v.memset(rw_u[:, :, 0:1], 0.0).then_inc(*step("rw_u0", L))
                v.tensor_copy(hg_K[:, :, :], hg_k[:, :, :])
                chain(v.memset(hg_att[:, :, :, :], 0.0))

                def keep_pairs(lev):
                    for t in range(NT):
                        now("hga_done", L, lev, t)
                        if lev >= 0:
                            now("hg_att", L, lev - 1, t)
                        b = ps[banks_of.get(("hga", L, lev, t), 0)]
                        if lev < 0:
                            v.copy_predicated(hg_att[:, t, :, :], ident().bitcast(I32).unsqueeze(1).to_broadcast([P, 4, P]),
                                              b[:, :].rearrange("p (h n) -> p h n", h=4)).then_inc(*step("hg_att", L, lev, t))
                        else:
                            hgt = HG_LEVELS[lev]
                            mask = of_tiles(cons[:, K_HG + lev:K_HG + lev + 1, :].bitcast(I32), hgt, 1).to_broadcast(
                                [P, 4, HALF // hgt, hgt])
                            v.copy_predicated(of_tiles(hg_att[:, t, :, :], hgt, 1), mask, bank_halves(b, hgt, 1)).then_inc(
                                *step("hg_att", L, lev, t))

                for lev in range(len(HG_LEVELS)):
                    hgt = HG_LEVELS[lev]
                    n = 2048 // (2 * hgt)
                    view = lambda t_: t_[:, :, :].rearrange("p h (n two s) -> p (h n) two s", two=2, s=hgt)
                    e0, e1 = [hg_decay(lev, i).rearrange("p (n s) -> p n s", s=hgt) for i in range(2)]
                    now("hg_ep", L, lev)
                    if lev:
                        now("hg_ex", L, lev)
                    chain(v.tensor_tensor(view(hg_x)[:, :, 0, :], view(hg_x)[:, :, 0, :],
                                          view(hg_p)[:, :, 1, hgt - 1:hgt].to_broadcast([P, n, hgt]), ALU.add))
                    v.tensor_tensor(view(hg_p)[:, :, 1, :], view(hg_p)[:, :, 1, :],
                                    view(hg_p)[:, :, 0, hgt - 1:hgt].to_broadcast([P, n, hgt]), ALU.add).then_inc(*step("hg_pupd", L, lev))
                    now("hg_pupd", L, lev)
                    if lev:
                        now("hga_done", L, lev - 1, NT - 1)
                        v.tensor_tensor(view(hg_K)[:, :, 0, :], view(hg_k)[:, :, 0, :], e1, ALU.mult)
                    v.tensor_tensor(view(hg_Q)[:, :, 1, :], view(hg_q)[:, :, 1, :], e0, ALU.mult).then_inc(*step("hg_K", L, lev))
                    keep_pairs(lev - 1)
                    if lev == 4:
                        lora_mix(L)
                keep_pairs(len(HG_LEVELS) - 1)
                now("hg_expX", L)
                now("hg_expP", L)
                now("hga_done", L, len(HG_LEVELS) - 1, NT - 1)
                v.tensor_tensor(hg_Q[:, :, :], hg_q[:, :, :], hg_p[:, :, :], ALU.mult)
                v.tensor_copy(lbT[:, 8:24].rearrange("p (h t) -> p h t", h=4),
                              hg_p[:, :, :].rearrange("p h (t n) -> p h t n", n=P)[:, :, :, P - 1]).then_inc(*step("hg_glast", L))
                v.tensor_tensor(hg_K[:, :, :], hg_k[:, :, :], hg_x[:, :, :], ALU.mult).then_inc(*step("hg_K", L, 99))
                now("hg_K", L, 99)
                first = prepare_dve(v, now, chain, L, 0)
                for t in range(NT - 1):
                    next(first)
                    next(first)
                    now("hgd_done", L, t)
                    b = ps[banks_of.get(("hgd", L, t), 0)]
                    for h in range(4):
                        if t == 0:
                            v.tensor_copy(hg_S[:, 1, h, :], b[:, h * P:(h + 1) * P]).then_inc(*step("hg_state", L, t, h))
                        else:
                            v.scalar_tensor_tensor(hg_S[:, t + 1, h, :], hg_S[:, t, h, :], lbT[:, 8 + 4 * h + t:9 + 4 * h + t],
                                                   b[:, h * P:(h + 1) * P], ALU.mult, ALU.add).then_inc(*step("hg_state", L, t, h))
                    now("hg_state", L, t, 3)
                hr = gn_small("hg_r")
                for t in range(NT):
                    now("hg_osq", L, t)
                    v.tensor_reduce(hr[:, t, :], hg_e[:, t % 2, 0:512].rearrange("p (h n) -> p h n", h=4), AX.X, ALU.add).then_inc(
                        *step("hg_ms0", L, t))
                    now("hg_ms0", L, t)
                    v.tensor_scalar(hr[:, t, :], hr[:, t, :], HG_EPS * P, None, ALU.add).then_inc(*step("hg_ms", L, t))
                now("hg_sqrt", L)
                chain(v.reciprocal(hr, hr))
                now("hg_row_in", L)
                for t in range(NT):
                    o = hg_o_buf(t)
                    b = ps[banks_of.get(("hgo", L, t), 0)]
                    v.tensor_tensor(o.rearrange("p (h n) -> p h n", h=4), b[:, :].rearrange("p (h n) -> p h n", h=4),
                                    hr[:, t, :].unsqueeze(2).to_broadcast([P, 4, P]), ALU.mult).then_inc(*step("hg_o", L, t))
                    now("hg_o", L, t)
                    chain(v.tensor_tensor(o, o, hg_row[:, :], ALU.mult))
                    now("hg_in", L, 3, t)
                    v.tensor_tensor(o, o, hg_g[:, t, :], ALU.mult).then_inc(*step("hg_ytok", L, t))

                for _ in first:
                    pass
                chain(v.memset(rk_sel[:, :, :], 0.0))
                for hd in range(2):
                    ins = v.tensor_copy(rk_sel[unit(hd), :, hd], parT[unit(hd), R_RK:R_RK + 4])
                ins.then_inc(*step("rk_sel", L))
                for ft in range(4):
                    core_dve(v, now, chain, L, ft)
                variance_dve(v, now, chain, L, 3)
                gated_dve(v, now, chain, L, 3)

                now("rw_yT", L, 3)
                for half in range(2):
                    for br in range(3):
                        if half or br:
                            now("dense_done", "branch", L, *divmod(3 * half + br - 1, 3), 3)
                        for k in range(4):
                            chain(v.tensor_copy(yT[0][:, k, :], y_raw[:, br, k, :]))
                            v.tensor_tensor(yT[1][:, k, :], y_raw[:, br, k, :], yT[0][:, k, :].bitcast(F32), ALU.subtract).then_inc(
                                *step("yT_rest", L, half, br, k))
                        for m in range(4):
                            now("gate_sig", L, half, br, m)
                            now("dense_done", "branch", L, half, br, m)
                            b = ps[banks_of.get(("branch", L, half, br, m), 0)]
                            dst = m_acc[:, 4 * half + m, :]
                            v.tensor_tensor(dst if br == 0 else m_tmp[:, :], gate_s[:, m, :], b[:, :], ALU.mult).then_inc(
                                *step("merge", L, half, br, m))
                            now("merge", L, half, br, m)
                            if br:
                                chain(v.tensor_tensor(dst, dst, m_tmp[:, :], ALU.add))
                            if br == 2:
                                k = 4 * half + m
                                chain(v.tensor_copy(mT[0][:, k, :], dst))
                                v.tensor_tensor(mT[1][:, k, :], dst, mT[0][:, k, :].bitcast(F32), ALU.subtract).then_inc(
                                    *step("mT_rest", L, k))
                now("h_back", L)
                residual("out", L, 1, ())
                norm(L, 1)
                ffn(L, 1)
                norm(L, 2)
                for half in range(2):
                    for m in range(4):
                        now("ple_sig", L, half, m)
                        now("dense_done", "pproj", L, half, m)
                        b = ps[banks_of.get(("pproj", L, half, m), 0)]
                        z = h_tok[:, m, 512 * half:512 * half + 512]
                        v.tensor_tensor(ple_pr[:, :], ple_sig[:, m, :], b[:, :], ALU.mult).then_inc(*step("ple_mul", L, half, m))
                        now("ple_mul", L, half, m)
                        v.tensor_tensor(z, z, ple_pr[:, :], ALU.add).then_inc(*step("res_sum", L, 3, half, m))
                        if half:
                            normalise(L, 3, m)
                        else:
                            stats(L, 3, m, 0)
                norm(L, 3, last=L == DEPTH - 1)



INPUTS = ["x", "p", "ln_g", "ln_b", "ffn1_wg", "ffn1_wu", "ffn1_wd", "w_in", "rw_mu", "rw_w0", "rw_w_up", "rw_a0",
          "rw_a_up", "rw_g_up", "rw_k_k", "rw_k_a", "rw_r_k", "rw_gn_g", "rw_gn_b", "hg_lb_raw", "hg_norm_g",
          "w_br_rw", "w_br_sb", "w_br_hg", "w_out", "ffn2_wg", "ffn2_wu", "ffn2_wd", "ple_gate", "ple_proj"]


def program(make, arrays):
    counts, banks_of = {}, {}
    for _ in range(2):
        nc = make()
        a = {n: nc.dram_tensor(f"in_{n}", v.shape, F32, kind="ExternalInput").ap() for n, v in arrays.items()}
        out = nc.dram_tensor("out_0_dram", (1, SEQ, D), F32, kind="ExternalOutput").ap()
        build(nc, a, out, counts, banks_of)
    return nc


def kernel(**inputs):
    import concourse.bacc as _bacc
    from concourse.bass_utils import run_bass_kernel_spmd as _run

    arrays = {n: np.ascontiguousarray(inputs[n]) for n in INPUTS}
    arrays["consts"] = constants()
    nc = program(lambda: _bacc.Bacc("TRN2", target_bir_lowering=False, num_devices=1), arrays)
    r = _run(nc, [{f"in_{n}": v for n, v in arrays.items()}], core_ids=[0])
    return r.results[0]["out_0_dram"]
```
